# Optimizing a Trainium2 kernel written in Bass

```python
import math
import jax, jax.numpy as jnp
from jax import lax
import numpy as np

D_MODEL = 2048
BATCH = 1
SEQ = 256
DEPTH = 2

N_MEM = 256
HEAD_DIM = 128
MEM_HEADS = 4
MEM_WIDTH = MEM_HEADS * HEAD_DIM
LRU_WIDTH = D_MODEL - MEM_WIDTH
LRU_BLOCKS = LRU_WIDTH // HEAD_DIM
CONV_WIDTH = 4
LRU_C = 8.0
DIL_GROUPS = ((128, 1), (512, 4), (2048, 16))
DIL_WIDTH = D_MODEL - MEM_WIDTH
DIL_HEADS = DIL_WIDTH // HEAD_DIM
HEADS_PER_GROUP = DIL_HEADS // len(DIL_GROUPS)
D_FF = -(-8 * D_MODEL // (3 * 256)) * 256
Q_BLOCK = 128
N_A = DEPTH // 2
N_B = DEPTH - N_A
RMS_EPS = 1e-6
NEG_INF = -1e30

kernel_name = "yoco_rglru_dilated_swa_hybrid"

def rms_norm(x, g):
    xf = x.astype(jnp.float32)
    y = xf * lax.rsqrt(jnp.mean(xf * xf, axis=-1, keepdims=True) + RMS_EPS)
    return (y * g.astype(jnp.float32)).astype(x.dtype)

def swiglu_sublayer(h, pre_g, post_g, w_ffn_in, w_ffn_out):
    hn = rms_norm(h, pre_g)
    gu = hn @ w_ffn_in
    g, u = gu[..., :D_FF], gu[..., D_FF:]
    y = (jax.nn.silu(g) * u) @ w_ffn_out
    return h + rms_norm(y, post_g)

def memory_attention(q_flat, mem_n, w_mem_kv):
    bsz, s, _ = q_flat.shape
    q = q_flat.reshape(bsz, s, MEM_HEADS, HEAD_DIM)
    kv = mem_n @ w_mem_kv
    m = kv.shape[1]
    k = kv[..., :MEM_WIDTH].reshape(bsz, m, MEM_HEADS, HEAD_DIM)
    v = kv[..., MEM_WIDTH:].reshape(bsz, m, MEM_HEADS, HEAD_DIM)
    sc = jnp.einsum('bshd,bmhd->bhsm', q, k).astype(jnp.float32) * (HEAD_DIM ** -0.5)
    p = jax.nn.softmax(sc, axis=-1).astype(v.dtype)
    o = jnp.einsum('bhsm,bmhd->bshd', p, v)
    return o.reshape(bsz, s, MEM_WIDTH)

def causal_depthwise_conv(x, w, b):
    c = x.shape[-1]
    y = lax.conv_general_dilated(x, w[:, None, :], window_strides=(1,),
                                 padding=((CONV_WIDTH - 1, 0),),
                                 dimension_numbers=('NWC', 'WIO', 'NWC'),
                                 feature_group_count=c)
    return y + b

def _linear_recurrence_combine(c1, c2):
    a1, b1 = c1
    a2, b2 = c2
    return a1 * a2, a2 * b1 + b2

def rg_lru(x, w_a, b_a, w_x, b_x, lam):
    bsz, s, c = x.shape
    xb = x.reshape(bsz, s, LRU_BLOCKS, HEAD_DIM)
    r = jax.nn.sigmoid(jnp.einsum('bsnc,ncd->bsnd', xb, w_a).reshape(bsz, s, c) + b_a)
    i = jax.nn.sigmoid(jnp.einsum('bsnc,ncd->bsnd', xb, w_x).reshape(bsz, s, c) + b_x)
    log_a = -LRU_C * r.astype(jnp.float32) * jax.nn.softplus(-lam.astype(jnp.float32))
    a = jnp.exp(log_a)
    bterm = jnp.sqrt(-jnp.expm1(2.0 * log_a)) * (i * x).astype(jnp.float32)
    _, h = lax.associative_scan(_linear_recurrence_combine, (a, bterm), axis=1)
    return h.astype(x.dtype)

def alibi_slopes(n):
    return jnp.exp2(-8.0 * (jnp.arange(n, dtype=jnp.float32) + 1.0) / n)

def dilated_group_attention(q, k, v, window, dil, slopes):
    bsz, s, h, dh = q.shape
    span = dil * Q_BLOCK
    sp = -(-s // span) * span
    sub_len = sp // dil
    nb = sub_len // Q_BLOCK
    pad = ((0, 0), (0, sp - s), (0, 0), (0, 0))

    def to_blocks(t):
        t = jnp.pad(t, pad).reshape(bsz, sub_len, dil, h, dh).transpose(0, 2, 1, 3, 4)
        return t.reshape(bsz, dil, nb, Q_BLOCK, h, dh)

    def with_prev(t):
        prev = jnp.pad(t, ((0, 0), (0, 0), (1, 0), (0, 0), (0, 0), (0, 0)))[:, :, :-1]
        return jnp.concatenate([prev, t], axis=3)

    qb = to_blocks(q)
    kb = with_prev(to_blocks(k))
    vb = with_prev(to_blocks(v))
    sc = jnp.einsum('brnqhd,brnkhd->brnhqk', qb, kb).astype(jnp.float32) * (dh ** -0.5)

    qi = jnp.arange(Q_BLOCK)[:, None]
    ki = jnp.arange(2 * Q_BLOCK)[None, :]
    rel = qi + Q_BLOCK - ki
    key_pos = jnp.arange(nb)[:, None, None] * Q_BLOCK - Q_BLOCK + ki[None]
    n_keys = window // dil
    valid = (rel >= 0)[None] & (rel <= n_keys)[None] & (key_pos >= 0)
    bias = -slopes[:, None, None] * (rel * dil).astype(jnp.float32)[None]
    sc = jnp.where(valid[:, None], sc + bias, NEG_INF)

    mx = jnp.max(sc, axis=-1, keepdims=True)
    lse = mx + jnp.log(jnp.sum(jnp.exp(sc - mx), axis=-1, keepdims=True))
    p = jnp.exp(sc - lse).astype(v.dtype)
    out = jnp.einsum('brnhqk,brnkhd->brnqhd', p, vb)
    out = out.reshape(bsz, dil, sub_len, h, dh).transpose(0, 2, 1, 3, 4).reshape(bsz, sp, h, dh)[:, :s]
    lse = lse[..., 0].transpose(0, 1, 2, 4, 3).reshape(bsz, dil, sub_len, h)
    lse = lse.transpose(0, 2, 1, 3).reshape(bsz, sp, h)[:, :s]
    return out, lse

def dilated_mixture_attention(q, k_shared, v_shared):
    slopes = alibi_slopes(DIL_HEADS)
    outs, lses = [], []
    for g, (window, dil) in enumerate(DIL_GROUPS):
        hs = slice(g * HEADS_PER_GROUP, (g + 1) * HEADS_PER_GROUP)
        o, l = dilated_group_attention(q[:, :, hs], k_shared[:, :, hs], v_shared[:, :, hs],
                                       window, dil, slopes[hs])
        outs.append(o)
        lses.append(l)
    w = jax.nn.softmax(jnp.stack(lses, axis=0), axis=0)
    comb = jnp.concatenate([outs[g] * w[g][..., None].astype(outs[g].dtype)
                            for g in range(len(DIL_GROUPS))], axis=2)
    bsz, s = q.shape[:2]
    return comb.reshape(bsz, s, DIL_WIDTH)

def recurrent_layer(h, mem_n, pre_mix_g, post_mix_g, pre_ffn_g, post_ffn_g, w_in, conv_w, conv_b,
                    gate_a_w, gate_a_b, gate_x_w, gate_x_b, lam, w_mem_kv, w_out, w_ffn_in, w_ffn_out):
    hn = rms_norm(h, pre_mix_g)
    proj = hn @ w_in
    xb = proj[..., :LRU_WIDTH]
    gb = proj[..., LRU_WIDTH:2 * LRU_WIDTH]
    qm = proj[..., 2 * LRU_WIDTH:]
    xc = causal_depthwise_conv(xb, conv_w, conv_b)
    y = rg_lru(xc, gate_a_w, gate_a_b, gate_x_w, gate_x_b, lam) * jax.nn.gelu(gb)
    m = memory_attention(qm, mem_n, w_mem_kv)
    mix = jnp.concatenate([y, m], axis=-1) @ w_out
    h = h + rms_norm(mix, post_mix_g)
    return swiglu_sublayer(h, pre_ffn_g, post_ffn_g, w_ffn_in, w_ffn_out)

def dilated_layer(h, mem_n, k_shared, v_shared, pre_mix_g, post_mix_g, pre_ffn_g, post_ffn_g,
                  w_in, w_mem_kv, w_out, w_ffn_in, w_ffn_out):
    bsz, s, _ = h.shape
    hn = rms_norm(h, pre_mix_g)
    proj = hn @ w_in
    q = proj[..., :DIL_WIDTH].reshape(bsz, s, DIL_HEADS, HEAD_DIM)
    a = dilated_mixture_attention(q, k_shared, v_shared)
    m = memory_attention(proj[..., DIL_WIDTH:], mem_n, w_mem_kv)
    mix = jnp.concatenate([a, m], axis=-1) @ w_out
    h = h + rms_norm(mix, post_mix_g)
    return swiglu_sublayer(h, pre_ffn_g, post_ffn_g, w_ffn_in, w_ffn_out)

def setup_inputs(seed: int = 0) -> dict:
    key = jax.random.key(seed)
    keys = iter(jax.random.split(key, 64))
    f32 = jnp.float32
    D = D_MODEL

    def nrm(shape, scale):
        return jax.random.normal(next(keys), shape, f32) * scale

    def gain(shape):
        return 1.0 + nrm(shape, 0.05)

    a0 = jax.random.uniform(next(keys), (N_A, LRU_WIDTH), f32, 0.9, 0.999)
    sig_l = a0 ** (1.0 / LRU_C)
    lam = jnp.log(sig_l) - jnp.log1p(-sig_l)

    return {
        "x": nrm((BATCH, SEQ, D), 1.0),
        "mem": nrm((BATCH, N_MEM, D), 1.0),
        "mem_norm_g": gain((D,)),
        "a_pre_mix_g": gain((N_A, D)),
        "a_post_mix_g": gain((N_A, D)),
        "a_pre_ffn_g": gain((N_A, D)),
        "a_post_ffn_g": gain((N_A, D)),
        "a_w_in": nrm((N_A, D, 2 * LRU_WIDTH + MEM_WIDTH), D ** -0.5),
        "a_conv_w": nrm((N_A, CONV_WIDTH, LRU_WIDTH), CONV_WIDTH ** -0.5),
        "a_conv_b": nrm((N_A, LRU_WIDTH), 0.02),
        "a_gate_a_w": nrm((N_A, LRU_BLOCKS, HEAD_DIM, HEAD_DIM), HEAD_DIM ** -0.5),
        "a_gate_a_b": nrm((N_A, LRU_WIDTH), 0.1),
        "a_gate_x_w": nrm((N_A, LRU_BLOCKS, HEAD_DIM, HEAD_DIM), HEAD_DIM ** -0.5),
        "a_gate_x_b": nrm((N_A, LRU_WIDTH), 0.1),
        "a_lambda": lam,
        "a_w_mem_kv": nrm((N_A, D, 2 * MEM_WIDTH), D ** -0.5),
        "a_w_out": nrm((N_A, LRU_WIDTH + MEM_WIDTH, D), (LRU_WIDTH + MEM_WIDTH) ** -0.5),
        "a_w_ffn_in": nrm((N_A, D, 2 * D_FF), D ** -0.5),
        "a_w_ffn_out": nrm((N_A, D_FF, D), D_FF ** -0.5),
        "kv_norm_g": gain((D,)),
        "w_kv_shared": nrm((D, 2 * DIL_WIDTH), D ** -0.5),
        "b_pre_mix_g": gain((N_B, D)),
        "b_post_mix_g": gain((N_B, D)),
        "b_pre_ffn_g": gain((N_B, D)),
        "b_post_ffn_g": gain((N_B, D)),
        "b_w_in": nrm((N_B, D, DIL_WIDTH + MEM_WIDTH), D ** -0.5),
        "b_w_mem_kv": nrm((N_B, D, 2 * MEM_WIDTH), D ** -0.5),
        "b_w_out": nrm((N_B, DIL_WIDTH + MEM_WIDTH, D), (DIL_WIDTH + MEM_WIDTH) ** -0.5),
        "b_w_ffn_in": nrm((N_B, D, 2 * D_FF), D ** -0.5),
        "b_w_ffn_out": nrm((N_B, D_FF, D), D_FF ** -0.5),
    }

def reference(x, mem, mem_norm_g, a_pre_mix_g, a_post_mix_g, a_pre_ffn_g, a_post_ffn_g, a_w_in,
              a_conv_w, a_conv_b, a_gate_a_w, a_gate_a_b, a_gate_x_w, a_gate_x_b, a_lambda,
              a_w_mem_kv, a_w_out, a_w_ffn_in, a_w_ffn_out, kv_norm_g, w_kv_shared,
              b_pre_mix_g, b_post_mix_g, b_pre_ffn_g, b_post_ffn_g, b_w_in, b_w_mem_kv, b_w_out,
              b_w_ffn_in, b_w_ffn_out):
    bsz, s, _ = x.shape
    mem_n = rms_norm(mem, mem_norm_g)
    h = x
    k_shared = v_shared = None
    for l in range(DEPTH):
        if l < N_A:
            h = recurrent_layer(h, mem_n, a_pre_mix_g[l], a_post_mix_g[l], a_pre_ffn_g[l],
                                a_post_ffn_g[l], a_w_in[l], a_conv_w[l], a_conv_b[l],
                                a_gate_a_w[l], a_gate_a_b[l], a_gate_x_w[l], a_gate_x_b[l],
                                a_lambda[l], a_w_mem_kv[l], a_w_out[l], a_w_ffn_in[l],
                                a_w_ffn_out[l])
            if l == N_A - 1:
                kv = rms_norm(h, kv_norm_g) @ w_kv_shared
                k_shared = kv[..., :DIL_WIDTH].reshape(bsz, s, DIL_HEADS, HEAD_DIM)
                v_shared = kv[..., DIL_WIDTH:].reshape(bsz, s, DIL_HEADS, HEAD_DIM)
        else:
            j = l - N_A
            h = dilated_layer(h, mem_n, k_shared, v_shared, b_pre_mix_g[j], b_post_mix_g[j],
                              b_pre_ffn_g[j], b_post_ffn_g[j], b_w_in[j], b_w_mem_kv[j],
                              b_w_out[j], b_w_ffn_in[j], b_w_ffn_out[j])
    return h


_drawn_inputs = setup_inputs


def setup_inputs(seed=0):
    import zlib

    import numpy as np

    out = dict(_drawn_inputs(seed))
    spreads = {}
    factors = {'mem_norm_g': 3.181, 'a_gate_a_b': 2.701, 'a_gate_x_b': 3.347, 'kv_norm_g': 7.348}
    for name, (base, spread) in spreads.items():
        noise = np.random.default_rng([zlib.crc32(name.encode()), seed]).standard_normal(out[name].shape)
        drawn = base * np.exp(spread * noise) if base else spread * noise
        out[name] = __import__('jax').numpy.asarray(drawn.astype(out[name].dtype))
    for name, factor in factors.items():
        out[name] = (out[name] * factor).astype(out[name].dtype)
    return out
```

```python
from contextlib import ExitStack

import concourse.bass as bass
import numpy as np
from concourse import mybir

F32 = mybir.dt.float32
F32R = mybir.dt.float32r
ALU = mybir.AluOpType
ACT = mybir.ActivationFunctionType
AX = mybir.AxisListType

P = 128
D = 2048
SEQ = 256
N_MEM = 256
TT = SEQ // P
KT = D // P
HEADS_M = 4
HEADS_D = 12
LRU_BLOCKS = 12
TAPS = 4
D_FF = 5632
FKT = D_FF // P
COLS = 512
FT = COLS // P
UK = 2
UNIT = UK * COLS
RING = 4
CU = KT // UK
FCU = FKT // UK
EPS = 1e-6
SCALE = float(P) ** -0.5
LRU_C = 8.0
DIL = (1, 4, 16)
GROUPS = len(DIL)
PER_GROUP = HEADS_D // GROUPS
FAR = 1e30

MIX_ORDER = [12, 13, 14, 15] + list(range(12))

STAGES = (("memA", 2, CU), ("memB", 2, CU), ("qmA", 1, CU), ("xg", 6, CU), ("outA", 4, CU),
          ("ffn_inA", 22, CU), ("ffn_outA", 4, FCU), ("qmB", 1, CU), ("kv", 6, CU), ("qB", 3, CU),
          ("outB", 4, CU), ("ffn_inB", 22, CU), ("ffn_outB", 4, FCU))
UNIT0, CHUNK0 = {}, {}
_u = _c = 0
for _name, _chunks, _units in STAGES:
    UNIT0[_name], CHUNK0[_name] = _u, _c
    _u += _chunks * _units
    _c += _chunks
N_UNITS = _u


class Sems:

    def __init__(self, sem):
        self.consts_in = sem("consts_in")
        self.gates_in = sem("gates_in")
        self.mem_in = sem("mem_in")
        self.x_in = sem("x_in")
        self.post_g_in = sem("post_g_in")
        self.out_stored = sem("out_stored")
        self.hi_done = sem("hi_done")
        self.lo_done = sem("lo_done")
        self.unit_used = sem("unit_used")
        self.chunk_drained = sem("chunk_drained")
        self.y_scaled = sem("y_scaled")
        self.sq_summed = sem("sq_summed")
        self.var_ready = sem("var_ready")
        self.std_ready = sem("std_ready")
        self.rstd_ready = sem("rstd_ready")
        self.h_new = sem("h_new")
        self.hn_ready = sem("hn_ready")
        self.tp_ready = sem("tp_ready")
        self.t_ready = sem("t_ready")
        self.xhi_ready = sem("xhi_ready")
        self.xT_ready = sem("xT_ready")
        self.pads_zero = sem("pads_zero")
        self.lru_abs = sem("lru_abs")
        self.lru_ez = sem("lru_ez")
        self.lru_c = sem("lru_c")
        self.conv_done = sem("conv_done")
        self.gates_done = sem("gates_done")
        self.gates_drained = sem("gates_drained")
        self.decay_ready = sem("decay_ready")
        self.ratio_ready = sem("ratio_ready")
        self.sqrt_done = sem("sqrt_done")
        self.scan_y = sem("scan_y")
        self.y_hi = sem("y_hi")
        self.y_ready = sem("y_ready")
        self.mid_hi_done = sem("mid_hi_done")
        self.mid_lo_done = sem("mid_lo_done")
        self.att_s = sem("att_s")
        self.att_mx = sem("att_mx")
        self.att_exp = sem("att_exp")
        self.att_p = sem("att_p")
        self.att_pt = sem("att_pt")
        self.att_ptc = sem("att_ptc")
        self.att_o = sem("att_o")
        self.m_hi = sem("m_hi")
        self.m_ready = sem("m_ready")
        self.dil_s = sem("dil_s")
        self.dil_mx = sem("dil_mx")
        self.dil_exp = sem("dil_exp")
        self.dil_p = sem("dil_p")
        self.dil_pt = sem("dil_pt")
        self.dil_ptc = sem("dil_ptc")
        self.dil_o = sem("dil_o")
        self.d_hi = sem("d_hi")
        self.d_ready = sem("d_ready")
        self.dve_step = sem("dve_step")
        self.far_in = sem("far_in")


def units_by(c):
    for name, chunks, units in STAGES:
        if c <= CHUNK0[name] + chunks:
            return UNIT0[name] + units * (c - CHUNK0[name])

NORM_GAINS = (1, 1, 1, 2, 1)
GROUP0 = [4 * n for n in range(5)]
TURN0 = [4 * sum(NORM_GAINS[:n]) for n in range(5)]


def build(nc, stream, x, mem, gains, lru, gate_w, post_g, dist, ident_in, out):
    with ExitStack() as ctx:
        def sb(name, shape, dt=F32):
            return ctx.enter_context(nc.sbuf_tensor(name, shape, dt))

        S = Sems(lambda name: ctx.enter_context(nc.semaphore(name)))
        landed = [ctx.enter_context(nc.semaphore(f"landed{s}")) for s in range(RING)]

        raw = sb("raw", [P, RING, UNIT])
        w_hi = sb("w_hi", [P, RING, UNIT], F32R)
        w_lo = sb("w_lo", [P, RING, UNIT], F32R)
        h = sb("h", [P, TT, D])
        piece = sb("piece", [P, 2, TT * COLS])
        kT_B = sb("kT_B", [P, HEADS_M, N_MEM])
        v_B = sb("v_B", [P, 2, COLS])
        ident = sb("identity", [P, P])
        gain = sb("gain", [P, 6, KT])
        lr = sb("lr", [P, 8, LRU_BLOCKS])
        lc = sb("lc", [P, 8, LRU_BLOCKS])
        st = sb("st", [P, 64])

        x_size, m_size = 2 * KT * SEQ * 4, 2 * FKT * SEQ * 4
        x_at = (nc.sbuf_base + 31) // 32 * 32
        sb("area", [P, (x_size + m_size) // 4])
        m_at = x_at + x_size

        def at(name, shape, offset, dt=F32):
            return nc.alloc_sbuf_tensor_at(name, shape, dt, offset=offset)

        half = KT * SEQ * 4
        xT_hi = at("xT_hi", [P, KT, SEQ], x_at, F32R)
        xT_lo = at("xT_lo", [P, KT, SEQ], x_at + half, F32R)
        yg = at("yg", [P, TT, D], x_at)
        pg = at("pg", [P, D], x_at + 16384)
        scrap = at("scrap", [P, D], x_at + 24576)
        dS = at("dS", [P, 2, GROUPS * 384], x_at)
        dPT = at("dPT", [P, GROUPS, 384], x_at + 9216)
        mix_hi = at("mix_hi", [P, KT, SEQ], m_at, F32R)
        mix_lo = at("mix_lo", [P, KT, SEQ], m_at + half, F32R)
        o = m_at + 2 * half
        kT_A = at("kT_A", [P, HEADS_M, N_MEM], o)
        v_A = at("v_A", [P, 2, COLS], o + 4096)
        q_A = at("q_A", [P, HEADS_M, SEQ], o + 8192)
        gw = at("gw", [P, 2 * LRU_BLOCKS, P], o + 12288)
        xbp = at("xbp", [P, FT, SEQ + TAPS - 1], o + 24576)
        o2 = o + 24576 + 4352
        xc, rr, ii, aa, bb, ge = (at(n, [P, FT, SEQ], o2 + 4096 * k)
                                  for k, n in enumerate(("xc", "rr", "ii", "aa", "bb", "ge")))
        kT_D = at("kT_D", [P, HEADS_D, SEQ], o)
        v_D = at("v_D", [P, TT, HEADS_D * P], o + 12288)
        q_D = at("q_D", [P, HEADS_D, SEQ], o + 24576)
        q_B = at("q_B", [P, HEADS_M, SEQ], o + 36864)
        far = at("far", [P, GROUPS, 2 * P], o + 40960)
        mid_hi = at("mid_hi", [P, FKT, SEQ], m_at, F32R)
        mid_lo = at("mid_lo", [P, FKT, SEQ], m_at + FKT * SEQ * 4, F32R)

        gemm_ps = [ctx.enter_context(nc.psum_tensor(f"gemm_ps{i}", [P, 1024], F32)) for i in range(2)]
        side_ps = [ctx.enter_context(nc.psum_tensor(f"side_ps{i}", [P, 1024], F32)) for i in range(2)]

        block = ctx.enter_context(nc.Block())

        def norm_plan(n):
            to_x, to_m = (xT_hi, xT_lo), (mix_hi, mix_lo)
            return ((yg, ((0, *to_m),)), (h, ((1, *to_x),)), (h, ((2, *to_x),)),
                    (h, ((3, *to_x), (4, *to_m))), (h, ((5, *to_x),)))[n]

        def ssq(n):
            return st[:, 2 * n:2 * n + 2]

        def rstd(n):
            return st[:, 10 + 2 * n:12 + 2 * n]

        def y_ssq(layer_stage):
            return st[:, 32:40]

        def y_rstd():
            return st[:, 40:42]

        mx, nmx, zz, rz = st[:, 44:46], st[:, 46:48], st[:, 48:50], st[:, 50:52]

        @block.sync
        def _(sp):
            for s in range(RING):
                sp.dma_start(raw[:, s, :], stream[s]).then_inc(landed[s], 16)
            with sp.Fori(1, N_UNITS // RING) as i:
                for s in range(RING):
                    sp.wait_ge(S.lo_done, i * RING + (s + 1 - RING))
                    sp.dma_start(raw[:, s, :], stream[bass.ds(i * RING + s, 1)].rearrange("a p n -> (a p) n")
                                 ).then_inc(landed[s], 16)
            for t in range(TT):
                sp.wait_ge(S.h_new, 3 * TT + t + 1)
                sp.dma_start(out[t * P:(t + 1) * P, :], h[:, t, :]).then_inc(S.out_stored, 16)
            sp.wait_ge(S.out_stored, 16 * TT)

        @block.gpsimd
        def _(pool):
            pool.dma_start(ident[:], ident_in).then_inc(S.consts_in, 16)
            pool.dma_start(gain[:].rearrange("p a b -> p (a b)"), gains).then_inc(S.consts_in, 16)
            pool.dma_start(lr[:].rearrange("p a b -> p (a b)"), lru).then_inc(S.consts_in, 16)
            pool.memset(xbp[:, :, 0:TAPS - 1], 0.0).then_inc(S.pads_zero, 1)
            pool.dma_start(gw[:].rearrange("p a b -> p (a b)"), gate_w).then_inc(S.gates_in, 16)
            for n, name in enumerate(("outA", "ffn_outA", "outB", "ffn_outB")):
                pool.wait_ge(S.unit_used, UNIT0["qB" if name == "outB" else name])
                pool.dma_start(pg[:], post_g[n:n + 1, :].to_broadcast([P, D])).then_inc(S.post_g_in, 16)
                if name == "ffn_outA":
                    pool.wait_ge(S.unit_used, UNIT0["qmB"])
                    pool.dma_start(far[:].rearrange("p a b -> p (a b)"), dist).then_inc(S.far_in, 16)

        @block.tensor
        def _(pe):
            def unit(n, slot, feature, acts, kts, first, last, pair):
                a_hi, a_lo = acts
                acc = gemm_ps[pair]
                pe.wait_ge(S.lo_done, n + 1)
                for k, kt in enumerate(kts):
                    tiles = FT if feature else TT
                    for t in range(tiles):
                        w = slice(k * COLS + (t * P if feature else 0), k * COLS + (t * P + P if feature else COLS))
                        for part, (w_part, a_part) in enumerate(((w_hi, a_hi), (w_hi, a_lo), (w_lo, a_hi))):
                            begin = first and k == 0 and part == 0
                            end = last and k == UK - 1 and part == 2
                            if feature:
                                mm = pe.matmul(acc[:, t * SEQ:(t + 1) * SEQ], w_part[:, slot, w], a_part[:, kt, :],
                                               start=begin and t % 2 == 0, stop=end, skip_group_check=True)
                            else:
                                mm = pe.matmul(acc[:, t * COLS:(t + 1) * COLS], a_part[:, kt, t * P:(t + 1) * P],
                                               w_part[:, slot, w], start=begin, stop=end)
                mm.then_inc(S.unit_used, 1)
                return mm

            def chunk(n, c, base, pair, feature, acts, kts, before=None, after=None):
                if not isinstance(c, int) or c >= 2:
                    pe.wait_ge(S.chunk_drained, c - 1)
                units = len(kts) // UK
                for u in range(units):
                    if before:
                        before(u)
                    unit(n + u, (base + u) % RING, feature, acts, kts[UK * u:UK * u + UK], u == 0,
                         u == units - 1, pair)
                    if after and u % RING == RING - 1:
                        after(u // RING)

            def wait_xT(norm, g=0):
                def before(u):
                    if u % 2 == 0:
                        pe.wait_ge(S.xT_ready, TURN0[norm] + NORM_GAINS[norm] * (u // 2) + g + 1)
                return before

            def norm_transposes(n):
                if n == 0:
                    pe.wait_ge(S.consts_in, 48)
                for q in range(4):
                    pe.wait_ge(S.hn_ready, GROUP0[n] + q + 1)
                    if GROUP0[n] + q >= 2:
                        m, qq = (n, q - 2) if q >= 2 else (n - 1, q + 2)
                        pe.wait_ge(S.t_ready, TURN0[m] + NORM_GAINS[m] * (qq + 1))
                    for k in range(4):
                        for t in range(TT):
                            tr = pe.transpose(side_ps[q % 2][:, k * SEQ + t * P:k * SEQ + (t + 1) * P],
                                              piece[:, q % 2, t * COLS + k * P:t * COLS + (k + 1) * P], ident[:])
                    tr.then_inc(S.tp_ready, 1)

            def mem_head(layer, head, step):
                q, kT, v = ((q_A, kT_A, v_A), (q_B, kT_B, v_B))[layer]
                n = HEADS_M * layer + head
                ps = side_ps[0]
                if step == 0:
                    if head == 0:
                        pe.wait_ge(S.chunk_drained, CHUNK0[("qmA", "qmB")[layer]] + 1)
                    if n:
                        pe.wait_ge(S.m_ready, n)
                    for t in range(TT):
                        mm = pe.matmul(ps[:, t * N_MEM:(t + 1) * N_MEM], q[:, head, t * P:(t + 1) * P],
                                       kT[:, head, :], start=True, stop=True)
                    mm.then_inc(S.att_s, 1)
                elif step == 1:
                    pe.wait_ge(S.att_p, n + 1)
                    for k in range(2):
                        for t in range(TT):
                            mm = pe.transpose(ps[:, COLS + k * SEQ + t * P:COLS + k * SEQ + (t + 1) * P],
                                              piece[:, 0, t * N_MEM + k * P:t * N_MEM + (k + 1) * P], ident[:])
                    mm.then_inc(S.att_pt, 1)
                else:
                    pe.wait_ge(S.att_ptc, n + 1)
                    for k in range(2):
                        mm = pe.matmul(ps[:, 0:SEQ], v[:, k, head * P:(head + 1) * P],
                                       piece[:, 1, k * SEQ:(k + 1) * SEQ], start=k == 0, stop=k == 1)
                    mm.then_inc(S.att_o, 1)

            def gates(j, part):
                if part == 0:
                    pe.wait_ge(S.conv_done, j + 1)
                if j + part:
                    pe.wait_ge(S.gates_drained, 2 * j + part)
                for g in range(2):
                    for b in range(2):
                        block_n = FT * j + 2 * part + b
                        mm = pe.matmul(side_ps[1][:, g * COLS + b * SEQ:g * COLS + (b + 1) * SEQ],
                                       gw[:, LRU_BLOCKS * g + block_n, :], xc[:, 2 * part + b, :],
                                       start=True, stop=True)
                mm.then_inc(S.gates_done, 1)

            def dil_scores(i):
                e = i % 2
                if i >= 2:
                    pe.wait_ge(S.d_ready, GROUPS * (i - 1))
                for g in range(GROUPS):
                    head = PER_GROUP * g + i
                    pe.matmul(side_ps[e][:, g * P:(g + 1) * P], q_D[:, head, 0:P], kT_D[:, head, 0:P],
                              start=True, stop=True)
                    mm = pe.matmul(gemm_ps[e][:, g * SEQ:(g + 1) * SEQ], q_D[:, head, P:SEQ], kT_D[:, head, :],
                                   start=True, stop=True)
                mm.then_inc(S.dil_s, 1)

            def dil_pt_ps(e, g):
                return (side_ps[e][:, 512:896], side_ps[e][:, 0:384], gemm_ps[e][:, 0:384])[g]

            def dil_o_ps(e, g):
                return (gemm_ps[e][:, 768:1024], gemm_ps[e][:, 0:256], side_ps[e][:, 0:256])[g]

            def dil_values(i):
                e = i % 2
                pe.wait_ge(S.dil_p, i + 1)
                for g in range(GROUPS):
                    ps = dil_pt_ps(e, g)
                    pe.transpose(ps[:, 0:P], dS[:, e, g * P:(g + 1) * P], ident[:])
                    for k in range(2):
                        mm = pe.transpose(ps[:, (1 + k) * P:(2 + k) * P],
                                          dS[:, e, 384 + g * SEQ + k * P:384 + g * SEQ + (k + 1) * P], ident[:])
                    mm.then_inc(S.dil_pt, 1)
                for g in range(GROUPS):
                    head = PER_GROUP * g + i
                    n = GROUPS * i + g
                    pe.wait_ge(S.dil_ptc, GROUPS * i + (GROUPS if g else 1))
                    o_ps = dil_o_ps(e, g)
                    pe.matmul(o_ps[:, 0:P], v_D[:, 0, head * P:(head + 1) * P], dPT[:, g, 0:P],
                              start=True, stop=True)
                    for k in range(2):
                        mm = pe.matmul(o_ps[:, P:SEQ], v_D[:, k, head * P:(head + 1) * P],
                                       dPT[:, g, (1 + k) * P:(2 + k) * P], start=k == 0, stop=k == 1)
                    mm.then_inc(S.dil_o, 1)

            def pair_of(c):
                return c % 2

            k_all = list(range(KT))
            x_acts, m_acts, mid_acts = (xT_hi, xT_lo), (mix_hi, mix_lo), (mid_hi, mid_lo)

            norm_transposes(0)
            for layer in range(2):
                for c in range(2):
                    u0, c0 = UNIT0["memA"] + CU * (2 * layer + c), 2 * layer + c
                    if layer == 1 and c == 1:
                        norm_transposes(1)
                    chunk(u0, c0, u0, pair_of(c0), c == 0, m_acts, k_all,
                          before=wait_xT(0) if c0 == 0 else None)

            u0, c0 = UNIT0["qmA"], CHUNK0["qmA"]
            chunk(u0, c0, u0, pair_of(c0), True, x_acts, k_all, before=wait_xT(1))
            for c in range(6):
                def after(half, c=c):
                    slot = 2 * c + half
                    mem_head(0, slot // 3, slot % 3)
                    if slot % 4 == 3:
                        if slot // 4 == 0:
                            pe.wait_ge(S.gates_in, 16)
                        gates(slot // 4, 0)
                        if slot == 11:
                            gates(2, 1)
                    elif slot % 4 == 0 and slot:
                        gates(slot // 4 - 1, 1)
                u0, c0 = UNIT0["xg"] + CU * c, CHUNK0["xg"] + c
                chunk(u0, c0, u0, pair_of(c0), True, x_acts, k_all, after=after)

            def wait_mix_A(u):
                if u == 0:
                    pe.wait_ge(S.m_ready, HEADS_M)
                elif u % 2 == 0:
                    pe.wait_ge(S.y_ready, u // 2)

            def wait_mix_B(u):
                if u == 0:
                    pe.wait_ge(S.m_ready, 2 * HEADS_M)
                    pe.wait_ge(S.d_ready, HEADS_D)

            def out_projection(name, waits):
                u0, c0 = UNIT0[name], CHUNK0[name]
                with pe.Fori(0, 2) as i:
                    for c in range(2):
                        chunk(i * (2 * CU) + (u0 + CU * c), i * 2 + (c0 + c), u0, pair_of(c0 + c), False, m_acts,
                              MIX_ORDER, before=waits if c == 0 else None)

            def ffn(layer, norm):
                name = "ffn_in" + layer
                u0, c0 = UNIT0[name], CHUNK0[name]
                with pe.Fori(0, 11) as i:
                    for c in range(2):
                        chunk(i * (2 * CU) + (u0 + CU * c), i * 2 + (c0 + c), u0, pair_of(c0 + c), True, x_acts,
                              k_all, before=wait_xT(norm) if c == 0 else None)
                name = "ffn_out" + layer
                u0, c0 = UNIT0[name], CHUNK0[name]
                first_pair = 11 * "AB".index(layer)

                def wait_mid(u):
                    if u % 2 == 0:
                        pe.wait_ge(S.mid_lo_done, first_pair + u // 2 + 1)
                with pe.Fori(0, 2) as i:
                    for c in range(2):
                        chunk(i * (2 * FCU) + (u0 + FCU * c), i * 2 + (c0 + c), u0 + FCU * c, pair_of(c0 + c), False,
                              mid_acts, list(range(FKT)), before=wait_mid if c == 0 else None)

            out_projection("outA", wait_mix_A)
            norm_transposes(2)
            ffn("A", 2)
            norm_transposes(3)

            u0, c0 = UNIT0["qmB"], CHUNK0["qmB"]
            chunk(u0, c0, u0, pair_of(c0), True, m_acts, k_all, before=wait_xT(3, 1))
            for c in range(6):
                def after(half, c=c):
                    slot = 2 * c + half
                    mem_head(1, slot // 3, slot % 3)
                u0, c0 = UNIT0["kv"] + CU * c, CHUNK0["kv"] + c
                chunk(u0, c0, u0, pair_of(c0), c < 3, x_acts, k_all, after=None)
            for c in range(3):
                u0, c0 = UNIT0["qB"] + CU * c, CHUNK0["qB"] + c
                chunk(u0, c0, u0, pair_of(c0), True, m_acts, k_all)
            for head in range(HEADS_M):
                for step in range(3):
                    mem_head(1, head, step)
            pe.wait_ge(S.chunk_drained, CHUNK0["outB"])
            pe.wait_ge(S.m_ready, 2 * HEADS_M)
            dil_scores(0)
            for i in range(PER_GROUP):
                if i + 1 < PER_GROUP:
                    dil_scores(i + 1)
                dil_values(i)

            out_projection("outB", wait_mix_B)
            norm_transposes(4)
            ffn("B", 4)

        def tp(q):
            return side_ps[q % 2][:, :]

        @block.scalar
        def _(act):
            def split(n, slot, first_use=False):
                act.wait_ge(landed[slot], n_landed(n, slot))
                if not first_use:
                    act.wait_ge(S.unit_used, n + (1 - RING))
                act.activation(w_hi[:, slot, :], raw[:, slot, :], ACT.Copy).then_inc(S.hi_done, 1)

            def n_landed(n, slot):
                if isinstance(n, int):
                    return 16 * (n // RING + 1)
                return n * 4 + (16 - 4 * slot)

            def split_range(n0, count):
                turns = count // RING if count > 2 * RING else 0
                if turns:
                    with act.Fori(0, turns) as i:
                        for u in range(RING):
                            split(i * RING + (n0 + u), (n0 + u) % RING)
                for n in range(n0 + turns * RING, n0 + count):
                    split(n, n % RING, n < RING)

            def norm_squares(n):
                src, _ = norm_plan(n)
                for t in range(TT):
                    if n + t:
                        act.wait_ge(S.sq_summed, TT * n + t)
                    if n == 0:
                        act.wait_ge(S.mem_in, 16 * TT)
                    elif n == 1:
                        act.wait_ge(S.x_in, 16 * TT)
                    else:
                        act.wait_ge(S.h_new, {2: 0, 3: TT, 4: 2 * TT}[n] + t + 1)
                    act.activation(scrap[:], src[:, t, :], ACT.Square, accum_out=ssq(n)[:, t:t + 1]
                                   ).then_inc(S.sq_summed, 1)

            def norm_std(k):
                act.wait_ge(S.var_ready, k + 1)
                act.activation(st[:, 56:58], st[:, 54:56], ACT.Sqrt).then_inc(S.std_ready, 1)

            def norm_rows(n):
                src, targets = norm_plan(n)
                act.wait_ge(S.rstd_ready, n + 1)

                if n:
                    act.wait_ge(S.xT_ready, TURN0[n])

                def rows(q):
                    for t in range(TT):
                        ins = act.activation(piece[:, q % 2, t * COLS:(t + 1) * COLS],
                                             src[:, t, q * COLS:(q + 1) * COLS], ACT.Copy, scale=rstd(n)[:, t:t + 1])
                    ins.then_inc(S.hn_ready, 1)

                def hi(q):
                    for g, (_, hi_to, _) in enumerate(targets):
                        turn = TURN0[n] + len(targets) * q + g
                        act.wait_ge(S.t_ready, turn + 1)
                        act.activation(hi_to[:, 4 * q:4 * q + 4, :].rearrange("p a b -> p (a b)"), piece[:, q % 2, :],
                                       ACT.Copy).then_inc(S.xhi_ready, 1)
                for q in range(4):
                    if q >= 2:
                        act.wait_ge(S.xT_ready, TURN0[n] + len(targets) * (q - 1))
                    rows(q)
                    if q:
                        hi(q - 1)
                hi(3)

            def drain(c, dst):
                act.wait_ge(S.unit_used, units_by(c + 1))
                act.activation(dst, gemm_ps[c % 2][:], ACT.Copy).then_inc(S.chunk_drained, 1)

            def flat(ap):
                return ap.rearrange("p a b -> p (a b)")

            def y_squares(name, c):
                k = {"outA": 0, "ffn_outA": 4, "outB": 8, "ffn_outB": 12}[name] + c
                act.wait_ge(S.y_scaled, k + 1)
                act.wait_ge(S.sq_summed, {"outA": 2, "ffn_outA": 3, "outB": 4, "ffn_outB": 5}[name] * TT)
                act.wait_ge(S.chunk_drained, CHUNK0[name] + c)
                for t in range(TT):
                    ins = act.activation(scrap[:, t * COLS:(t + 1) * COLS], gemm_ps[(CHUNK0[name] + c) % 2][:, t * COLS:(t + 1) * COLS],
                                         ACT.Square, accum_out=y_ssq(name)[:, 2 * c + t:2 * c + t + 1])
                ins.then_inc(S.chunk_drained, 1)

            def mem_softmax(layer, head):
                n = HEADS_M * layer + head
                act.wait_ge(S.att_mx, n + 1)
                for t in range(TT):
                    ins = act.activation(piece[:, 0, t * N_MEM:(t + 1) * N_MEM],
                                         side_ps[0][:, t * N_MEM:(t + 1) * N_MEM], ACT.Exp,
                                         bias=nmx[:, t:t + 1], scale=SCALE, accum_out=zz[:, t:t + 1])
                ins.then_inc(S.att_exp, 1)

            def mem_react(layer, slot):
                head, stp = slot // 3, slot % 3
                n = HEADS_M * layer + head
                if stp == 0:
                    mem_softmax(layer, head)
                elif stp == 1:
                    act.wait_ge(S.att_pt, n + 1)
                    act.activation(piece[:, 1, 0:COLS], side_ps[0][:, COLS:2 * COLS], ACT.Copy).then_inc(S.att_ptc, 1)
                else:
                    act.wait_ge(S.att_o, n + 1)
                    act.activation(mix_hi[:, 12 + head, :], side_ps[0][:, 0:SEQ], ACT.Copy).then_inc(S.m_hi, 1)

            def gate_sigmoids(j, part):
                act.wait_ge(S.gates_done, 2 * j + part + 1)
                if part == 0 and j:
                    act.wait_ge(S.y_ready, j)
                for g, dst in enumerate((rr, ii)):
                    for b in range(2):
                        k = 2 * part + b
                        ins = act.activation(dst[:, k, :], side_ps[1][:, g * COLS + b * SEQ:g * COLS + (b + 1) * SEQ],
                                             ACT.Sigmoid, bias=lr[:, 5 + g, FT * j + k:FT * j + k + 1])
                ins.then_inc(S.gates_drained, 1)

            def lru_act(j):
                act.wait_ge(S.gates_drained, 2 * j + 2)
                if j == 0:
                    act.wait_ge(S.lru_c, 1)
                for b in range(FT):
                    k = FT * j + b
                    act.activation(bb[:, b, :], rr[:, b, :], ACT.Tanh, scale=lc[:, 1, k:k + 1])
                    act.activation(aa[:, b, :], rr[:, b, :], ACT.Exp, scale=lc[:, 0, k:k + 1]).then_inc(S.decay_ready, 1)
                act.wait_ge(S.ratio_ready, j + 1)
                act.activation(flat(rr[:]), flat(bb[:]), ACT.Sqrt, scale=2.0).then_inc(S.sqrt_done, 1)
                act.wait_ge(S.scan_y, j + 1)
                act.activation(flat(mix_hi[:, FT * j:FT * j + FT, :]), flat(ii[:]), ACT.Copy).then_inc(S.y_hi, 1)

            def copy_xb(j, c):
                act.wait_ge(S.unit_used, units_by(c + 1))
                if j:
                    act.wait_ge(S.conv_done, j)
                act.activation(xbp[:, :, TAPS - 1:], gemm_ps[c % 2][:].rearrange("p (a b) -> p a b", a=FT), ACT.Copy
                               ).then_inc(S.chunk_drained, 1)

            def gelu(j, c):
                act.wait_ge(S.unit_used, units_by(c + 1))
                act.activation(flat(ge[:]), gemm_ps[c % 2][:], ACT.Gelu_apprx_tanh).then_inc(S.chunk_drained, 1)

            for t in range(TT):
                act.dma_start(yg[:, t, :], mem[t * P:(t + 1) * P, :]).then_inc(S.mem_in, 16)
            for t in range(TT):
                act.dma_start(h[:, t, :], x[t * P:(t + 1) * P, :]).then_inc(S.x_in, 16)
            norm_squares(0)
            norm_squares(1)
            norm_std(0)
            norm_rows(0)
            act.wait_ge(S.lru_abs, 1)
            act.activation(lc[:, 2, :], lc[:, 2, :], ACT.Exp, scale=-1.0).then_inc(S.lru_ez, 1)
            norm_std(1)

            mem_dst = (flat(kT_A[:]), flat(v_A[:]), flat(kT_B[:]), flat(v_B[:]))
            for c in range(4):
                n0 = CU * c
                split_range(n0, 4)
                if c:
                    drain(c - 1, mem_dst[c - 1])
                if c == 3:
                    norm_rows(1)
                split_range(n0 + 4, 4)
            n0 = UNIT0["qmA"]
            split_range(n0, 4)
            drain(3, mem_dst[3])
            split_range(n0 + 4, 4)

            for g in range(13):
                split_range(UNIT0["xg"] + RING * g, RING)
                if g == 0:
                    drain(CHUNK0["qmA"], flat(q_A[:]))
                if g >= 1:
                    mem_react(0, g - 1)
                if g >= 2 and g % 2 == 0:
                    c = g // 2 - 1
                    (gelu if c % 2 else copy_xb)(c // 2, CHUNK0["xg"] + c)
                if g % 4 == 0 and g:
                    gate_sigmoids(g // 4 - 1, 0)
                if g % 4 == 1 and g > 1:
                    gate_sigmoids(g // 4 - 1, 1)
                    lru_act(g // 4 - 1)
                if g == 12:
                    gate_sigmoids(2, 1)
                    lru_act(2)
            split_range(UNIT0["outA"] + 4, 4)

            def token_stage(name, units):
                for c in range(1, 4):
                    n0 = UNIT0[name] + units * c
                    split_range(n0, 4)
                    y_squares(name, c - 1)
                    split_range(n0 + 4, units - 4)

            def post_norm(name, k, norm, next_unit):
                split_range(next_unit, 4)
                y_squares(name, 3)
                norm_std(k)
                norm_squares(norm)
                norm_std(k + 1)
                norm_rows(norm)

            def mid_hi_part(c, at_tile):
                act.wait_ge(S.chunk_drained, c)
                act.activation(flat(mid_hi[:, at_tile, :]), piece[:, 1, :], ACT.Copy).then_inc(S.mid_hi_done, 1)

            def ffn_in(layer):
                name = "ffn_in" + layer
                u0, c0 = UNIT0[name], CHUNK0[name]

                def one(i, peeled):
                    if not peeled:
                        for u in range(4):
                            split(i * 16 + (u0 + u), u)
                        mid_hi_part(i * 2 + c0, bass.ds(i * FT - FT, FT))
                    for u in range(4, 8):
                        split(i * 16 + (u0 + u), u % RING)
                    for u in range(8, 12):
                        split(i * 16 + (u0 + u), u % RING)
                    act.wait_ge(S.unit_used, i * 16 + (u0 + CU))
                    act.activation(piece[:, 0, :], gemm_ps[c0 % 2][:], ACT.Silu).then_inc(S.chunk_drained, 1)
                    for u in range(12, 16):
                        split(i * 16 + (u0 + u), u % RING)
                one(0, True)
                with act.Fori(1, 11) as i:
                    one(i, False)
                n0 = UNIT0["ffn_out" + layer]
                split_range(n0, 4)
                mid_hi_part(c0 + 22, slice(FKT - FT, FKT))
                split_range(n0 + 4, FCU - 4)

            token_stage("outA", CU)
            post_norm("outA", 2, 2, UNIT0["ffn_inA"])
            ffn_in("A")
            token_stage("ffn_outA", FCU)
            post_norm("ffn_outA", 4, 3, UNIT0["qmB"])

            split_range(UNIT0["qmB"] + 4, 4)
            dests = [flat(q_B[:])]
            dests += [flat(kT_D[:, FT * c:FT * c + FT, :]) for c in range(3)]
            dests += [v_D[:, :, c * COLS:(c + 1) * COLS] for c in range(3)]
            dests += [flat(q_D[:, FT * c:FT * c + FT, :]) for c in range(3)]
            for c in range(10):
                n0 = UNIT0["kv"] + CU * c
                split_range(n0, 4)
                if c in (4, 5, 6):
                    cc = CHUNK0["qmB"] + c
                    act.wait_ge(S.unit_used, units_by(cc + 1))
                    act.activation(dests[c], gemm_ps[cc % 2][:].rearrange("p (t n) -> p t n", t=TT), ACT.Copy
                                   ).then_inc(S.chunk_drained, 1)
                else:
                    drain(CHUNK0["qmB"] + c, dests[c])
                if c < 9:
                    split_range(n0 + 4, 4)
            for slot in range(12):
                mem_react(1, slot)

            def dil_pt_ps(e, g):
                return (side_ps[e][:, 512:896], side_ps[e][:, 0:384], gemm_ps[e][:, 0:384])[g]

            def dil_o_ps(e, g):
                return (gemm_ps[e][:, 768:1024], gemm_ps[e][:, 0:256], side_ps[e][:, 0:256])[g]

            def dil_exp(i):
                e = i % 2
                act.wait_ge(S.dil_mx, i + 1)
                for t, cols in enumerate((slice(0, 384), slice(384, 1152))):
                    ins = act.activation(dS[:, e, cols], dS[:, e, cols], ACT.Exp, bias=nmx[:, t:t + 1], scale=SCALE,
                                         accum_out=zz[:, t:t + 1])
                ins.then_inc(S.dil_exp, 1)

            dil_exp(0)
            for i in range(PER_GROUP):
                e = i % 2
                for g in range(GROUPS):
                    act.wait_ge(S.dil_pt, GROUPS * i + g + 1)
                    if i:
                        act.wait_ge(S.dil_o, GROUPS * (i - 1) + g + 1)
                    act.activation(dPT[:, g, :], dil_pt_ps(e, g), ACT.Copy).then_inc(S.dil_ptc, 1)
                if i + 1 < PER_GROUP:
                    dil_exp(i + 1)
                for g in range(GROUPS):
                    act.wait_ge(S.dil_o, GROUPS * i + g + 1)
                    act.activation(mix_hi[:, PER_GROUP * g + i, :], dil_o_ps(e, g), ACT.Copy).then_inc(S.d_hi, 1)
            split_range(UNIT0["outB"] + 4, 4)
            token_stage("outB", CU)
            post_norm("outB", 6, 4, UNIT0["ffn_inB"])
            ffn_in("B")
            token_stage("ffn_outB", FCU)
            y_squares("ffn_outB", 3)
            norm_std(8)

        @block.vector
        def _(dve):
            steps = [0]

            def step(ins):
                steps[0] += 1
                ins.then_inc(S.dve_step, 1)
                dve.wait_ge(S.dve_step, steps[0])

            def flat(ap):
                return ap.rearrange("p a b -> p (a b)")

            def split(n, slot):
                dve.wait_ge(S.hi_done, n + 1)
                dve.tensor_tensor(w_lo[:, slot, :], raw[:, slot, :], w_hi[:, slot, :].bitcast(F32), ALU.subtract
                                  ).then_inc(S.lo_done, 1)

            def split_range(n0, count):
                turns = count // RING if count > 2 * RING else 0
                if turns:
                    with dve.Fori(0, turns) as i:
                        for u in range(RING):
                            split(i * RING + (n0 + u), (n0 + u) % RING)
                for n in range(n0 + turns * RING, n0 + count):
                    split(n, n % RING)

            def lo_part(dst, whole, hi):
                return dve.tensor_tensor(dst, whole, hi, ALU.subtract)

            def variance(src):
                dve.tensor_scalar(st[:, 54:56], src, 1.0 / D, EPS, ALU.mult, ALU.add).then_inc(S.var_ready, 1)

            def norm_var(n):
                dve.wait_ge(S.sq_summed, TT * (n + 1))
                variance(ssq(n))

            def norm_rstd(n, k):
                dve.wait_ge(S.std_ready, k + 1)
                dve.reciprocal(rstd(n), st[:, 56:58]).then_inc(S.rstd_ready, 1)

            def norm_turn(n):
                _, targets = norm_plan(n)
                for q in range(4):
                    dve.wait_ge(S.tp_ready, GROUP0[n] + q + 1)
                    for g, (row, hi_to, lo_to) in enumerate(targets):
                        turn = TURN0[n] + len(targets) * q + g
                        if g:
                            dve.wait_ge(S.xT_ready, turn)
                        dve.tensor_tensor(piece[:, q % 2, :].rearrange("p (a b) -> p a b", a=4),
                                          tp(q).rearrange("p (a b) -> p a b", a=4),
                                          gain[:, row, 4 * q:4 * q + 4].unsqueeze(2).to_broadcast([P, 4, SEQ]),
                                          ALU.mult).then_inc(S.t_ready, 1)
                        dve.wait_ge(S.xhi_ready, turn + 1)
                        lo_part(flat(lo_to[:, 4 * q:4 * q + 4, :]), piece[:, q % 2, :],
                                flat(hi_to[:, 4 * q:4 * q + 4, :]).bitcast(F32)).then_inc(S.xT_ready, 1)

            def y_scale(name, c):
                k = ("outA", "ffn_outA", "outB", "ffn_outB").index(name)
                cc = CHUNK0[name] + c
                dve.wait_ge(S.unit_used, units_by(cc + 1))
                dve.wait_ge(S.post_g_in, 16 * (k + 1))
                dve.tensor_tensor(yg[:, :, c * COLS:(c + 1) * COLS], gemm_ps[cc % 2][:].rearrange("p (t n) -> p t n", t=TT),
                                  pg[:, c * COLS:(c + 1) * COLS].unsqueeze(1).to_broadcast([P, TT, COLS]), ALU.mult
                                  ).then_inc(S.y_scaled, 1)

            def residual(name, k):
                dve.wait_ge(S.chunk_drained, CHUNK0[name] + 4)
                step(dve.tensor_reduce(st[:, 42:44], y_ssq(name).rearrange("p (c t) -> p t c", t=TT), AX.X, ALU.add))
                variance(st[:, 42:44])
                dve.wait_ge(S.std_ready, k + 1)
                step(dve.reciprocal(y_rstd(), st[:, 56:58]))
                for t in range(TT):
                    dve.scalar_tensor_tensor(h[:, t, :], yg[:, t, :], y_rstd()[:, t:t + 1], h[:, t, :], ALU.mult,
                                             ALU.add).then_inc(S.h_new, 1)

            def mem_react(layer, slot):
                head, stp = slot // 3, slot % 3
                n = HEADS_M * layer + head
                if stp == 0:
                    dve.wait_ge(S.att_s, n + 1)
                    step(dve.tensor_reduce(mx, side_ps[0][:, 0:COLS].rearrange("p (t n) -> p t n", t=TT), AX.X, ALU.max))
                    dve.tensor_scalar(nmx, mx, -SCALE, None, ALU.mult).then_inc(S.att_mx, 1)
                    dve.wait_ge(S.att_exp, n + 1)
                    step(dve.reciprocal(rz, zz))
                    for t in range(TT):
                        p = piece[:, 0, t * N_MEM:(t + 1) * N_MEM]
                        ins = dve.tensor_scalar(p, p, rz[:, t:t + 1], None, ALU.mult)
                    ins.then_inc(S.att_p, 1)
                elif stp == 2:
                    dve.wait_ge(S.m_hi, n + 1)
                    lo_part(mix_lo[:, 12 + head, :], side_ps[0][:, 0:SEQ], mix_hi[:, 12 + head, :].bitcast(F32)
                            ).then_inc(S.m_ready, 1)

            def conv(j):
                dve.wait_ge(S.chunk_drained, CHUNK0["xg"] + 2 * j + 1)
                if j == 0:
                    dve.wait_ge(S.pads_zero, 1)
                for k in range(TAPS - 1, -1, -1):
                    for b in range(FT):
                        n = FT * j + b
                        w = lr[:, k, n:n + 1]
                        src = xbp[:, b, k:k + SEQ]
                        if k == TAPS - 1:
                            ins = dve.tensor_scalar(xc[:, b, :], src, w, lr[:, 4, n:n + 1], ALU.mult, ALU.add)
                        else:
                            ins = dve.scalar_tensor_tensor(xc[:, b, :], src, w, xc[:, b, :], ALU.mult, ALU.add)
                    if k:
                        step(ins)
                ins.then_inc(S.conv_done, 1)

            def lru(j):
                dve.wait_ge(S.decay_ready, FT * (j + 1))
                step(dve.tensor_scalar(flat(rr[:]), flat(bb[:]), 1.0, None, ALU.add))
                step(dve.reciprocal(flat(rr[:]), flat(rr[:])))
                dve.scalar_tensor_tensor(flat(bb[:]), flat(bb[:]), 1e-30, flat(rr[:]), ALU.max, ALU.mult
                                         ).then_inc(S.ratio_ready, 1)
                step(dve.tensor_tensor(flat(ii[:]), flat(ii[:]), flat(xc[:]), ALU.mult))
                dve.wait_ge(S.sqrt_done, j + 1)
                step(dve.tensor_tensor(flat(bb[:]), flat(rr[:]), flat(ii[:]), ALU.mult))
                for b in range(FT):
                    ins = dve.tensor_tensor_scan(rr[:, b, :], aa[:, b, :], bb[:, b, :], 0.0, ALU.mult, ALU.add)
                step(ins)
                dve.wait_ge(S.chunk_drained, CHUNK0["xg"] + 2 * j + 2)
                dve.tensor_tensor(flat(ii[:]), flat(rr[:]), flat(ge[:]), ALU.mult).then_inc(S.scan_y, 1)
                dve.wait_ge(S.y_hi, j + 1)
                lo_part(flat(mix_lo[:, FT * j:FT * j + FT, :]), flat(ii[:]),
                        flat(mix_hi[:, FT * j:FT * j + FT, :]).bitcast(F32)).then_inc(S.y_ready, 1)

            def decay_constants():
                lam, z, s, s2, acc, t = (lr[:, 7, :], lc[:, 2, :], lc[:, 3, :], lc[:, 4, :], lc[:, 5, :], lc[:, 6, :])
                dve.wait_ge(S.lru_ez, 1)
                step(dve.tensor_scalar(t, z, 2.0, None, ALU.add))
                step(dve.reciprocal(t, t))
                step(dve.tensor_tensor(s, z, t, ALU.mult))
                step(dve.tensor_tensor(s2, s, s, ALU.mult))
                top = 17
                step(dve.tensor_scalar(acc, s2, 1.0 / top, 1.0 / (top - 2), ALU.mult, ALU.add))
                for k in range(top - 4, 0, -2):
                    step(dve.tensor_tensor(acc, acc, s2, ALU.mult))
                    step(dve.tensor_scalar(acc, acc, 1.0 / k, None, ALU.add))
                step(dve.tensor_tensor(acc, acc, s, ALU.mult))
                step(dve.tensor_scalar(t, lam, -1.0, 0.0, ALU.mult, ALU.max))
                step(dve.scalar_tensor_tensor(t, acc, 2.0, t, ALU.mult, ALU.add))
                step(dve.tensor_scalar(lc[:, 0, :], t, -LRU_C, None, ALU.mult))
                dve.tensor_scalar(lc[:, 1, :], t, LRU_C, None, ALU.mult).then_inc(S.lru_c, 1)

            dve.wait_ge(S.consts_in, 48)
            norm_var(0)
            norm_rstd(0, 0)
            lam = lr[:, 7, :]
            step(dve.tensor_scalar(lc[:, 7, :], lam, -1.0, None, ALU.mult))
            dve.tensor_tensor(lc[:, 2, :], lc[:, 7, :], lam, ALU.max).then_inc(S.lru_abs, 1)
            norm_turn(0)
            norm_var(1)
            norm_rstd(1, 1)
            decay_constants()
            for c in range(4):
                split_range(CU * c, 4)
                if c == 3:
                    norm_turn(1)
                split_range(CU * c + 4, 4)
            split_range(UNIT0["qmA"], 8)

            for g in range(13):
                split_range(UNIT0["xg"] + RING * g, RING)
                if g >= 1:
                    mem_react(0, g - 1)
                if g in (2, 6, 10):
                    conv(g // 4)
                if g % 4 == 1 and g > 1:
                    lru(g // 4 - 1)
                if g == 12:
                    lru(2)
            split_range(UNIT0["outA"] + 4, 4)

            def token_stage(name, units):
                for c in range(1, 4):
                    n0 = UNIT0[name] + units * c
                    split_range(n0, 4)
                    y_scale(name, c - 1)
                    split_range(n0 + 4, units - 4)

            def post_norm(name, k, norm, next_unit):
                split_range(next_unit, 4)
                y_scale(name, 3)
                residual(name, k)
                norm_var(norm)
                norm_rstd(norm, k + 1)
                norm_turn(norm)

            def ffn_in(layer):
                name = "ffn_in" + layer
                u0, c0 = UNIT0[name], CHUNK0[name]
                k0 = 11 * "AB".index(layer)

                def hidden(k, c, u, at_tile):
                    dve.wait_ge(S.chunk_drained, c - 1)
                    dve.wait_ge(S.unit_used, u)
                    if not isinstance(k, int) or k > 1:
                        dve.wait_ge(S.mid_lo_done, k - 1)
                    dve.tensor_tensor(piece[:, 1, :], piece[:, 0, :], gemm_ps[(c0 + 1) % 2][:], ALU.mult
                                      ).then_inc(S.chunk_drained, 1)
                    dve.wait_ge(S.mid_hi_done, k)
                    lo_part(flat(mid_lo[:, at_tile, :]), piece[:, 1, :], flat(mid_hi[:, at_tile, :]).bitcast(F32)
                            ).then_inc(S.mid_lo_done, 1)

                def one(i, peeled):
                    if not peeled:
                        for u in range(4):
                            split(i * 16 + (u0 + u), u)
                        hidden(i + k0, i * 2 + c0, i * 16 + u0,
                               slice(0, FT) if isinstance(i, int) else bass.ds(i * FT - FT, FT))
                    for u in range(4, 16):
                        split(i * 16 + (u0 + u), u % RING)
                one(0, True)
                one(1, False)
                with dve.Fori(2, 11) as i:
                    one(i, False)
                n0 = UNIT0["ffn_out" + layer]
                split_range(n0, 4)
                hidden(k0 + 11, c0 + 22, n0, slice(FKT - FT, FKT))
                split_range(n0 + 4, FCU - 4)

            token_stage("outA", CU)
            post_norm("outA", 2, 2, UNIT0["ffn_inA"])
            ffn_in("A")
            token_stage("ffn_outA", FCU)
            post_norm("ffn_outA", 4, 3, UNIT0["qmB"])

            split_range(UNIT0["qmB"] + 4, 10 * CU)
            for slot in range(12):
                mem_react(1, slot)

            def dil_o_ps(e, g):
                return (gemm_ps[e][:, 768:1024], gemm_ps[e][:, 0:256], side_ps[e][:, 0:256])[g]

            def dil_scores(i):
                e = i % 2
                dve.wait_ge(S.dil_s, i + 1)
                if i == 0:
                    dve.wait_ge(S.far_in, 16)
                if i >= 2:
                    dve.wait_ge(S.dil_pt, GROUPS * (i - 1))
                for g in range(GROUPS):
                    slope = -(2.0 ** (-8.0 * (PER_GROUP * g + i + 1) / HEADS_D)) / SCALE
                    dve.scalar_tensor_tensor(dS[:, e, g * P:(g + 1) * P], far[:, g, P:2 * P], slope,
                                             side_ps[e][:, g * P:(g + 1) * P], ALU.mult, ALU.add)
                    ins = dve.scalar_tensor_tensor(dS[:, e, 384 + g * SEQ:384 + (g + 1) * SEQ], far[:, g, :], slope,
                                                   gemm_ps[e][:, g * SEQ:(g + 1) * SEQ], ALU.mult, ALU.add)
                step(ins)
                dve.tensor_reduce(mx[:, 0:1], dS[:, e, 0:384], AX.X, ALU.max)
                step(dve.tensor_reduce(mx[:, 1:2], dS[:, e, 384:1152], AX.X, ALU.max))
                dve.tensor_scalar(nmx, mx, -SCALE, None, ALU.mult).then_inc(S.dil_mx, 1)

            def dil_norm(i):
                e = i % 2
                dve.wait_ge(S.dil_exp, i + 1)
                step(dve.reciprocal(rz, zz))
                for t, cols in enumerate((slice(0, 384), slice(384, 1152))):
                    ins = dve.tensor_scalar(dS[:, e, cols], dS[:, e, cols], rz[:, t:t + 1], None, ALU.mult)
                ins.then_inc(S.dil_p, 1)

            dil_scores(0)
            dil_norm(0)
            for i in range(PER_GROUP):
                e = i % 2
                if i + 1 < PER_GROUP:
                    dil_scores(i + 1)
                    dil_norm(i + 1)
                for g in range(GROUPS):
                    head = PER_GROUP * g + i
                    dve.wait_ge(S.d_hi, GROUPS * i + g + 1)
                    lo_part(mix_lo[:, head, :], dil_o_ps(e, g), mix_hi[:, head, :].bitcast(F32)).then_inc(S.d_ready, 1)
            split_range(UNIT0["outB"] + 4, 4)
            token_stage("outB", CU)
            post_norm("outB", 6, 4, UNIT0["ffn_inB"])
            ffn_in("B")
            token_stage("ffn_outB", FCU)
            y_scale("ffn_outB", 3)
            residual("ffn_outB", 8)


def tiles(w, k_order, cols):
    out = []
    for c in cols:
        block = w[:, c:c + COLS].reshape(-1, P, COLS)[k_order]
        block = block.reshape(-1, UK, P, COLS).transpose(0, 2, 1, 3)
        out.append(block.reshape(-1, P, UNIT))
    return out


def by_partition(v):
    return v.reshape(-1, P).T


def kernel(**inputs):
    import concourse.bacc as bacc
    from concourse.bass_utils import run_bass_kernel_spmd

    a = {k: np.asarray(v) for k, v in inputs.items()}
    d_all, f_all = list(range(KT)), list(range(FKT))
    units = []
    units += tiles(a["a_w_mem_kv"][0], d_all, (0, 512))
    units += tiles(a["b_w_mem_kv"][0], d_all, (0, 512))
    units += tiles(a["a_w_in"][0], d_all, (3072, 0, 1536, 512, 2048, 1024, 2560))
    units += tiles(a["a_w_out"][0], MIX_ORDER, range(0, D, COLS))
    pairs = [c for j in range(0, D_FF, COLS) for c in (j, D_FF + j)]
    units += tiles(a["a_w_ffn_in"][0], d_all, pairs)
    units += tiles(a["a_w_ffn_out"][0], f_all, range(0, D, COLS))
    units += tiles(a["b_w_in"][0], d_all, (1536,))
    units += tiles(a["w_kv_shared"], d_all, range(0, 3072, COLS))
    units += tiles(a["b_w_in"][0], d_all, (0, 512, 1024))
    units += tiles(a["b_w_out"][0], MIX_ORDER, range(0, D, COLS))
    units += tiles(a["b_w_ffn_in"][0], d_all, pairs)
    units += tiles(a["b_w_ffn_out"][0], f_all, range(0, D, COLS))
    stream = np.concatenate(units)

    gains = np.concatenate([by_partition(v) for v in (
        a["mem_norm_g"], a["a_pre_mix_g"][0], a["a_pre_ffn_g"][0], a["kv_norm_g"], a["b_pre_mix_g"][0],
        a["b_pre_ffn_g"][0])], axis=1)
    lru = np.concatenate([by_partition(v) for v in (
        *a["a_conv_w"][0], a["a_conv_b"][0], a["a_gate_a_b"][0], a["a_gate_x_b"][0], a["a_lambda"][0])], axis=1)
    gate_w = np.concatenate([a["a_gate_a_w"][0], a["a_gate_x_w"][0]]).transpose(1, 0, 2).reshape(P, -1)
    post_g = np.stack([a["a_post_mix_g"][0], a["a_post_ffn_g"][0], a["b_post_mix_g"][0], a["b_post_ffn_g"][0]])

    rel = np.arange(P)[:, None] + P - np.arange(2 * P)[None, :]
    dist = np.stack([np.where((rel >= 0) & (rel % d == 0) & ((rel <= P) if d == 1 else True), rel, FAR)
                     for d in DIL], axis=1).reshape(P, -1).astype(np.float32)
    arrays = {"stream": stream, "x": a["x"][0], "mem": a["mem"][0], "gains": gains, "lru": lru, "gate_w": gate_w,
              "post_g": post_g, "dist": dist, "ident": np.eye(P, dtype=np.float32)}
    arrays = {k: np.ascontiguousarray(v) for k, v in arrays.items()}

    nc = bacc.Bacc("TRN2", target_bir_lowering=False, num_devices=1)
    args = [nc.dram_tensor(k, v.shape, mybir.dt.from_np(v.dtype), kind="ExternalInput").ap() for k, v in arrays.items()]
    args.append(nc.dram_tensor("out", (SEQ, D), F32, kind="ExternalOutput").ap())
    build(nc, *args)
    r = run_bass_kernel_spmd(nc, [arrays], core_ids=[0])
    return r.results[0]["out"].reshape(1, SEQ, D)
```

```python
from contextlib import ExitStack

import concourse.bass as bass
import numpy as np
from concourse import mybir

F32 = mybir.dt.float32
F32R = mybir.dt.float32r
ALU = mybir.AluOpType
ACT = mybir.ActivationFunctionType
AX = mybir.AxisListType

P = 128
D = 2048
SEQ = 256
N_MEM = 256
TT = SEQ // P
KT = D // P
HEADS_M = 4
HEADS_D = 12
LRU_BLOCKS = 12
TAPS = 4
D_FF = 5632
FKT = D_FF // P
COLS = 512
FT = COLS // P
UK = 2
UNIT = UK * COLS
RING = 4
CU = KT // UK
FCU = FKT // UK
EPS = 1e-6
SCALE = float(P) ** -0.5
LRU_C = 8.0
DIL = (1, 4, 16)
GROUPS = len(DIL)
PER_GROUP = HEADS_D // GROUPS
FAR = 1e30

ORDER_A = [12, 13, 14, 15] + list(range(12))
TRIO_HEADS = [PER_GROUP * g + i for i in range(PER_GROUP) for g in range(GROUPS)]
ORDER_B = [12, 13, 14, 15] + TRIO_HEADS

DIL_S, DIL_PT, DIL_O = (33, 41, 49, 57), (37, 45, 53, 61), (66, 69, 73, 74)

XG = (("x", 0), ("g", 0), ("x", 1), ("x", 2), ("g", 1), ("g", 2))
LRU_AT = (11, 27, 37)
Y_AT = (25, 44, 51)

STAGES = (("memA", 2, CU), ("memB", 2, CU), ("qmA", 1, CU), ("xg", 6, CU), ("outA", 4, CU),
          ("ffn_inA", 22, CU), ("ffn_outA", 4, FCU), ("qmB", 1, CU), ("kB", 3, CU), ("qB", 3, CU), ("vB", 3, CU),
          ("outB", 4, CU), ("ffn_inB", 22, CU), ("ffn_outB", 4, FCU))
UNIT0, CHUNK0 = {}, {}
_u = _c = 0
for _name, _chunks, _units in STAGES:
    UNIT0[_name], CHUNK0[_name] = _u, _c
    _u += _chunks * _units
    _c += _chunks
N_UNITS = _u


class Sems:

    def __init__(self, sem):
        self.consts_in = sem("consts_in")
        self.gates_in = sem("gates_in")
        self.lru_in = sem("lru_in")
        self.x_in = sem("x_in")
        self.post_g_in = sem("post_g_in")
        self.out_stored = sem("out_stored")
        self.hi_done = sem("hi_done")
        self.lo_done = sem("lo_done")
        self.unit_used = sem("unit_used")
        self.chunk_drained = sem("chunk_drained")
        self.y_scaled = sem("y_scaled")
        self.sq_summed = sem("sq_summed")
        self.var_ready = sem("var_ready")
        self.std_ready = sem("std_ready")
        self.rstd_ready = sem("rstd_ready")
        self.diag_ready = sem("diag_ready")
        self.spread_done = sem("spread_done")
        self.spread_ready = sem("spread_ready")
        self.h_new = sem("h_new")
        self.hn_ready = sem("hn_ready")
        self.tp_ready = sem("tp_ready")
        self.xhi_ready = sem("xhi_ready")
        self.xT_ready = sem("xT_ready")
        self.pads_zero = sem("pads_zero")
        self.ones_set = sem("ones_set")
        self.tap_done = sem("tap_done")
        self.one_set = sem("one_set")
        self.lru_abs = sem("lru_abs")
        self.lru_ez = sem("lru_ez")
        self.lru_c = sem("lru_c")
        self.conv_done = sem("conv_done")
        self.gates_done = sem("gates_done")
        self.gates_drained = sem("gates_drained")
        self.decay_ready = sem("decay_ready")
        self.ratio_ready = sem("ratio_ready")
        self.sqrt_done = sem("sqrt_done")
        self.scan_done = sem("scan_done")
        self.scan_y = sem("scan_y")
        self.y_hi = sem("y_hi")
        self.y_ready = sem("y_ready")
        self.mid_hi_done = sem("mid_hi_done")
        self.silu_done = sem("silu_done")
        self.hid_ready = sem("hid_ready")
        self.mid_lo_done = sem("mid_lo_done")
        self.att_s = sem("att_s")
        self.att_mx = sem("att_mx")
        self.att_exp = sem("att_exp")
        self.att_p = sem("att_p")
        self.att_pt = sem("att_pt")
        self.att_ptc = sem("att_ptc")
        self.att_o = sem("att_o")
        self.m_hi = sem("m_hi")
        self.m_ready = sem("m_ready")
        self.dil_s = sem("dil_s")
        self.dil_mx = sem("dil_mx")
        self.dil_exp = sem("dil_exp")
        self.dil_p = sem("dil_p")
        self.dil_pt = sem("dil_pt")
        self.dil_ptc = sem("dil_ptc")
        self.dil_o = sem("dil_o")
        self.d_hi = sem("d_hi")
        self.d_ready = sem("d_ready")
        self.dve_step = sem("dve_step")
        self.far_in = sem("far_in")


def units_by(c):
    for name, chunks, units in STAGES:
        if c <= CHUNK0[name] + chunks:
            return UNIT0[name] + units * (c - CHUNK0[name])

NORM_GAINS = (1, 1, 1, 2, 1)
GROUP0 = [4 * n for n in range(5)]
TURN0 = [4 * sum(NORM_GAINS[:n]) for n in range(5)]
TOKEN_STAGES = ("outA", "ffn_outA", "outB", "ffn_outB")


def build(nc, stream, x, mem, gains, lru, gate_w, post_g, dist, ident_in, out):
    with ExitStack() as ctx:
        def sb(name, shape, dt=F32):
            return ctx.enter_context(nc.sbuf_tensor(name, shape, dt))

        S = Sems(lambda name: ctx.enter_context(nc.semaphore(name)))
        landed = [ctx.enter_context(nc.semaphore(f"landed{s}")) for s in range(RING)]

        raw = sb("raw", [P, RING, UNIT])
        w_hi = sb("w_hi", [P, RING, UNIT], F32R)
        w_lo = sb("w_lo", [P, RING, UNIT], F32R)
        h = sb("h", [P, TT, D])
        piece = sb("piece", [P, 2, TT * COLS])
        kv_B = sb("kv_B", [P, 2, HEADS_M * N_MEM])
        ident = sb("identity", [P, P])
        ones = sb("ones", [P, P])
        diag = sb("diag", [P, TT, P])
        spread = sb("spread", [P, SEQ])
        gain = sb("gain", [P, 6, KT])
        lr = sb("lr", [P, 8, LRU_BLOCKS])
        lc = sb("lc", [P, 8, LRU_BLOCKS])
        st = sb("st", [P, 64])

        x_size, m_size = 2 * KT * SEQ * 4, 2 * FKT * SEQ * 4
        x_at = (nc.sbuf_base + 31) // 32 * 32
        sb("area", [P, (x_size + m_size) // 4])
        m_at = x_at + x_size

        def at(name, shape, offset, dt=F32):
            return nc.alloc_sbuf_tensor_at(name, shape, dt, offset=offset)

        half = KT * SEQ * 4
        xT_hi = at("xT_hi", [P, KT, SEQ], x_at, F32R)
        xT_lo = at("xT_lo", [P, KT, SEQ], x_at + half, F32R)
        yg = at("yg", [P, 4, TT, COLS], x_at)
        pg = at("pg", [P, D], x_at + 16384)
        scrap = at("scrap", [P, D], x_at + 24576)
        d_hi = at("d_hi", [P, HEADS_D, SEQ], x_at, F32R)
        d_lo = at("d_lo", [P, HEADS_D, SEQ], x_at + 12288, F32R)
        mix_hi = at("mix_hi", [P, KT, SEQ], m_at, F32R)
        mix_lo = at("mix_lo", [P, KT, SEQ], m_at + half, F32R)
        o = m_at + 2 * half
        kT_A = at("kT_A", [P, HEADS_M, N_MEM], o)
        v_A = at("v_A", [P, 2, COLS], o + 4096)
        q_A = at("q_A", [P, HEADS_M, SEQ], o + 8192)
        gw = at("gw", [P, 2 * LRU_BLOCKS, P], o + 12288)
        xbp = at("xbp", [P, FT, SEQ + TAPS - 1], o + 24576)
        o2 = o + 24576 + 4352
        xc, rr, ii, aa, bb, ge = (at(n, [P, FT, SEQ], o2 + 4096 * k)
                                  for k, n in enumerate(("xc", "rr", "ii", "aa", "bb", "ge")))
        kT_D = at("kT_D", [P, HEADS_D, SEQ], o)
        v_D = at("v_D", [P, TT, HEADS_D * P], o + 12288)
        q_D = at("q_D", [P, HEADS_D, SEQ], o + 24576)
        far = at("far", [P, GROUPS, 2 * P], o + 36864)
        m_hi_B = at("m_hi_B", [P, HEADS_M, SEQ], o + 43008, F32R)
        m_lo_B = at("m_lo_B", [P, HEADS_M, SEQ], o + 47104, F32R)
        q_B = at("q_B", [P, HEADS_M, SEQ], o + 51200)
        yg_B = at("yg_B", [P, 4, TT, COLS], m_at)
        pg_B = at("pg_B", [P, D], m_at + 16384)
        scrap_B = at("scrap_B", [P, D], m_at + 24576)
        kT_B, v_B = kv_B[:, 0, :].rearrange("p (a b) -> p a b", a=HEADS_M), kv_B[:, 1, :].rearrange(
            "p (a b) -> p a b", a=2)
        kv_flat = kv_B[:].rearrange("p a b -> p (a b)")
        small = piece[:].rearrange("p a b -> p (a b)")
        dS = (kv_flat[:, 1152:1536], small[:, 1152:1920])
        dPT = (small[:, 0:1152], kv_flat[:, 0:1152], at("dPT2", [P, 1152], o + 51200)[:],
               at("dPT3", [P, 1152], x_at + 24576)[:])
        mid_hi = at("mid_hi", [P, FKT, SEQ], m_at, F32R)
        mid_lo = at("mid_lo", [P, FKT, SEQ], m_at + FKT * SEQ * 4, F32R)

        gemm_ps = [ctx.enter_context(nc.psum_tensor(f"gemm_ps{i}", [P, 1024], F32)) for i in range(2)]
        side_ps = [ctx.enter_context(nc.psum_tensor(f"side_ps{i}", [P, 1024], F32)) for i in range(2)]

        block = ctx.enter_context(nc.Block())

        def norm_plan(n):
            to_x, to_m = (xT_hi, xT_lo), (mix_hi, mix_lo)
            return ((yg, ((0, *to_m),)), (h, ((1, *to_x),)), (h, ((2, *to_x),)),
                    (h, ((4, *to_x), (3, *to_m))), (h, ((5, *to_x),)))[n]

        def token_buffers(name):
            return (yg_B, pg_B, scrap_B) if name == "outB" else (yg, pg, scrap)

        def ssq(n):
            return st[:, 2 * n:2 * n + 2]

        def rstd(n):
            return st[:, 10 + 2 * n:12 + 2 * n]

        def y_ssq(layer_stage):
            return st[:, 32:40]

        def y_rstd():
            return st[:, 40:42]

        mx, nmx, zz, rz = st[:, 44:46], st[:, 46:48], st[:, 48:50], st[:, 50:52]
        tiny, one, scrap1 = st[:, 60:61], st[:, 61:62], st[:, 62:63]
        mem_in = [ctx.enter_context(nc.semaphore(f"mem_in{q}")) for q in range(4)]

        def flat(ap):
            return ap.rearrange("p a b -> p (a b)")

        def head_slot(head):
            return TRIO_HEADS.index(head)

        def dil_scores_ps(g):
            return side_ps[1][:, g * P:(g + 1) * P], side_ps[0][:, g * SEQ:(g + 1) * SEQ]

        def dil_pt_ps(g):
            return (side_ps[1][:, 512:896], side_ps[0][:, 0:384], side_ps[1][:, 0:384])[g]

        def dil_o_ps(g):
            return (side_ps[0][:, 768:1024], side_ps[0][:, 0:256], side_ps[1][:, 0:256])[g]

        @block.sync
        def _(sp):
            for s in range(RING):
                cols = slice(s * COLS, (s + 1) * COLS)
                sp.dma_start(yg[:, s, :, :], mem[:, cols].rearrange("(t p) n -> p t n", p=P)).then_inc(mem_in[s], 16)
                sp.dma_start(raw[:, s, :], stream[s]).then_inc(landed[s], 16)
            with sp.Fori(1, N_UNITS // RING) as i:
                for s in range(RING):
                    sp.wait_ge(S.lo_done, i * RING + (s + 1 - RING))
                    sp.dma_start(raw[:, s, :], stream[bass.ds(i * RING + s, 1)].rearrange("a p n -> (a p) n")
                                 ).then_inc(landed[s], 16)
            for q in range(4):
                cols = slice(q * COLS, (q + 1) * COLS)
                sp.wait_ge(S.h_new, 3 * 4 * TT + TT * (q + 1))
                sp.dma_start(out[:, cols].rearrange("(t p) n -> p t n", p=P), h[:, :, cols]).then_inc(S.out_stored, 16)
            sp.wait_ge(S.out_stored, 16 * 4)

        @block.gpsimd
        def _(pool):
            pool.memset(ones[:], 1.0).then_inc(S.ones_set, 1)
            pool.dma_start(flat(lr[:]), lru).then_inc(S.lru_in, 16)
            pool.memset(xbp[:, :, 0:TAPS - 1], 0.0).then_inc(S.pads_zero, 1)
            pool.dma_start(flat(gw[:]), gate_w).then_inc(S.gates_in, 16)
            for n, name in enumerate(TOKEN_STAGES):
                pool.wait_ge(S.unit_used, UNIT0[name])
                pool.dma_start(token_buffers(name)[1][:], post_g[n:n + 1, :].to_broadcast([P, D])
                               ).then_inc(S.post_g_in, 16)
                if name == "ffn_outA":
                    pool.wait_ge(S.unit_used, UNIT0["qmB"])
                    pool.dma_start(flat(far[:]), dist).then_inc(S.far_in, 16)

        @block.tensor
        def _(pe):
            def unit(n, slot, feature, acts, kts, first, last, pair):
                acc = gemm_ps[pair]
                pe.wait_ge(S.lo_done, n + 1)
                for k, kt in enumerate(kts):
                    a_hi, a_lo = acts(kt)
                    for t in range(FT if feature else TT):
                        w = slice(k * COLS + (t * P if feature else 0), k * COLS + (t * P + P if feature else COLS))
                        for part, (w_part, a_part) in enumerate(((w_hi, a_hi), (w_hi, a_lo), (w_lo, a_hi))):
                            begin = first and k == 0 and part == 0
                            end = last and k == UK - 1 and part == 2
                            if feature:
                                mm = pe.matmul(acc[:, t * SEQ:(t + 1) * SEQ], w_part[:, slot, w], a_part,
                                               start=begin and t % 2 == 0, stop=end, skip_group_check=True)
                            else:
                                mm = pe.matmul(acc[:, t * COLS:(t + 1) * COLS], a_part[:, t * P:(t + 1) * P],
                                               w_part[:, slot, w], start=begin, stop=end)
                mm.then_inc(S.unit_used, 1)

            def chunk(n, c, base, pair, feature, acts, kts, before=None, after=None):
                if not isinstance(c, int) or c >= 2:
                    pe.wait_ge(S.chunk_drained, c - 1)
                units = len(kts) // UK
                for u in range(units):
                    if before:
                        before(u)
                    unit(n + u, (base + u) % RING, feature, acts, kts[UK * u:UK * u + UK], u == 0,
                         u == units - 1, pair)
                    if after:
                        after(u)

            def turn_group(n, q):
                src, _ = norm_plan(n)
                if n == 0:
                    if q == 0:
                        pe.wait_ge(S.consts_in, 32)
                    pe.wait_ge(mem_in[q], 16)
                elif n == 1:
                    pe.wait_ge(S.hn_ready, q + 1)
                    if q == 0:
                        pe.wait_ge(S.spread_ready, 1)
                else:
                    pe.wait_ge(S.h_new, 4 * TT * (n - 2) + TT * (q + 1))
                if GROUP0[n] + q >= 2:
                    m, qq = (n, q - 2) if q >= 2 else (n - 1, q + 2)
                    pe.wait_ge(S.xT_ready, TURN0[m] + NORM_GAINS[m] * (qq + 1))
                for k in range(4):
                    for t in range(TT):
                        rows = (piece[:, q % 2, t * COLS + k * P:t * COLS + (k + 1) * P] if n == 1 else
                                src[:, q, t, k * P:(k + 1) * P] if n == 0 else
                                src[:, t, (4 * q + k) * P:(4 * q + k + 1) * P])
                        tr = pe.transpose(side_ps[q % 2][:, k * SEQ + t * P:k * SEQ + (t + 1) * P], rows, ident[:])
                tr.then_inc(S.tp_ready, 1)

            def turns(n):
                def before(u):
                    if u == 0:
                        turn_group(n, 0)
                        turn_group(n, 1)
                    if u in (2, 4):
                        turn_group(n, u // 2 + 1)
                    if u % 2 == 0:
                        pe.wait_ge(S.xT_ready, TURN0[n] + NORM_GAINS[n] * (u // 2) + 1)
                return before

            def spread_rstd(n):
                if n == 0:
                    pe.wait_ge(S.ones_set, 1)
                k = (0, None, 1, 2, 3)[n]
                pe.wait_ge(S.diag_ready, k + 1)
                for t in range(TT):
                    mm = pe.matmul(side_ps[0][:, t * P:(t + 1) * P], ones[:], diag[:, t, :], start=True, stop=True)
                mm.then_inc(S.spread_done, 1)

            def mem_head(layer, head, step):
                q, kT, v = ((q_A, kT_A, v_A), (q_B, kT_B, v_B))[layer]
                n = HEADS_M * layer + head
                ps = side_ps[0]
                if step == 0:
                    if head == 0:
                        pe.wait_ge(S.chunk_drained, CHUNK0[("qmA", "qmB")[layer]] + 1)
                    if n:
                        pe.wait_ge(S.m_ready, n)
                    if layer == 1 and head == 0:
                        pe.wait_ge(S.spread_ready, 3)
                    for t in range(TT):
                        mm = pe.matmul(ps[:, t * N_MEM:(t + 1) * N_MEM], q[:, head, t * P:(t + 1) * P],
                                       kT[:, head, :], start=True, stop=True)
                    mm.then_inc(S.att_s, 1)
                elif step == 1:
                    pe.wait_ge(S.att_p, n + 1)
                    for k in range(2):
                        for t in range(TT):
                            mm = pe.transpose(ps[:, COLS + k * SEQ + t * P:COLS + k * SEQ + (t + 1) * P],
                                              piece[:, 0, t * N_MEM + k * P:t * N_MEM + (k + 1) * P], ident[:])
                    mm.then_inc(S.att_pt, 1)
                else:
                    pe.wait_ge(S.att_ptc, n + 1)
                    for k in range(2):
                        mm = pe.matmul(ps[:, 0:SEQ], v[:, k, head * P:(head + 1) * P],
                                       piece[:, 1, k * SEQ:(k + 1) * SEQ], start=k == 0, stop=k == 1)
                    mm.then_inc(S.att_o, 1)

            def gates(j, part):
                if part == 0:
                    pe.wait_ge(S.conv_done, j + 1)
                if j + part == 0:
                    pe.wait_ge(S.gates_in, 16)
                if j + part:
                    pe.wait_ge(S.gates_drained, 2 * j + part)
                for g in range(2):
                    for b in range(2):
                        block_n = FT * j + 2 * part + b
                        mm = pe.matmul(side_ps[1][:, g * COLS + b * SEQ:g * COLS + (b + 1) * SEQ],
                                       gw[:, LRU_BLOCKS * g + block_n, :], xc[:, 2 * part + b, :],
                                       start=True, stop=True)
                mm.then_inc(S.gates_done, 1)

            def dil_scores(i):
                pe.wait_ge(S.chunk_drained, CHUNK0["qB"] + min(i, 2) + 1)
                if i == 0:
                    pe.wait_ge(S.m_ready, 2 * HEADS_M)
                else:
                    pe.wait_ge(S.dil_ptc, GROUPS * i)
                for g in range(GROUPS):
                    head = PER_GROUP * g + i
                    q = q_D[:, head_slot(head), :]
                    ps0, ps1 = dil_scores_ps(g)
                    pe.matmul(ps0, q[:, 0:P], kT_D[:, head, 0:P], start=True, stop=True)
                    mm = pe.matmul(ps1, q[:, P:SEQ], kT_D[:, head, :], start=True, stop=True)
                mm.then_inc(S.dil_s, 1)

            def dil_turn(i):
                pe.wait_ge(S.dil_p, i + 1)
                for g in range(GROUPS):
                    ps = dil_pt_ps(g)
                    pe.transpose(ps[:, 0:P], dS[0][:, g * P:(g + 1) * P], ident[:])
                    for k in range(2):
                        mm = pe.transpose(ps[:, (1 + k) * P:(2 + k) * P],
                                          dS[1][:, g * SEQ + k * P:g * SEQ + (k + 1) * P], ident[:])
                    mm.then_inc(S.dil_pt, 1)

            def dil_values(i):
                pe.wait_ge(S.chunk_drained, CHUNK0["vB"] + min(i, 2) + 1)
                pe.wait_ge(S.dil_ptc, GROUPS * PER_GROUP)
                if i:
                    pe.wait_ge(S.d_ready, GROUPS * i)
                for g in range(GROUPS):
                    v = slice(head_slot(PER_GROUP * g + i) * P, (head_slot(PER_GROUP * g + i) + 1) * P)
                    pt = dPT[i][:, g * 384:(g + 1) * 384]
                    pe.matmul(dil_o_ps(g)[:, 0:P], v_D[:, 0, v], pt[:, 0:P], start=True, stop=True)
                    for k in range(2):
                        mm = pe.matmul(dil_o_ps(g)[:, P:SEQ], v_D[:, k, v], pt[:, (1 + k) * P:(2 + k) * P],
                                       start=k == 0, stop=k == 1)
                    mm.then_inc(S.dil_o, 1)

            def pair_of(c):
                return c % 2

            def tiles_of(hi, lo):
                return lambda kt: (hi[:, kt, :], lo[:, kt, :])

            k_all = list(range(KT))
            x_acts, m_acts, mid_acts = tiles_of(xT_hi, xT_lo), tiles_of(mix_hi, mix_lo), tiles_of(mid_hi, mid_lo)

            def mix_B(kt):
                if kt >= HEADS_D:
                    return m_hi_B[:, kt - HEADS_D, :], m_lo_B[:, kt - HEADS_D, :]
                return d_hi[:, head_slot(kt), :], d_lo[:, head_slot(kt), :]

            for c in range(4):
                def after(u, c=c):
                    n = CU * c + u
                    if n == CU - 1:
                        spread_rstd(0)
                    if n in (14, 16, 18, 20):
                        turn_group(1, (n - 14) // 2)
                chunk(CU * c, c, CU * c, pair_of(c), c % 2 == 0, m_acts, k_all, before=turns(0) if c == 0 else None,
                      after=after)

            u0, c0 = UNIT0["qmA"], CHUNK0["qmA"]
            pe.wait_ge(S.xT_ready, TURN0[2])
            chunk(u0, c0, u0, pair_of(c0), True, x_acts, k_all)
            for c in range(len(XG)):
                def after(u, c=c):
                    n = CU * c + u
                    if n % 2 == 0 and 2 <= n <= 24:
                        mem_head(0, (n // 2 - 1) // 3, (n // 2 - 1) % 3)
                    for j, at_unit in enumerate(LRU_AT):
                        if n == at_unit + 1:
                            gates(j, 0)
                        if n == at_unit + 3:
                            gates(j, 1)
                u0, c0 = UNIT0["xg"] + CU * c, CHUNK0["xg"] + c
                chunk(u0, c0, u0, pair_of(c0), True, x_acts, k_all, after=after)

            def wait_mix_A(u):
                if u == 0:
                    pe.wait_ge(S.m_ready, HEADS_M)
                elif u % 2 == 0:
                    pe.wait_ge(S.y_ready, u // 2)

            for c in range(4):
                u0, c0 = UNIT0["outA"] + CU * c, CHUNK0["outA"] + c
                chunk(u0, c0, u0, pair_of(c0), False, m_acts, ORDER_A, before=wait_mix_A if c == 0 else None)

            def ffn(layer, norm):
                name = "ffn_in" + layer
                u0, c0 = UNIT0[name], CHUNK0[name]
                chunk(u0, c0, u0, pair_of(c0), True, x_acts, k_all, before=turns(norm))
                spread_rstd(norm)
                chunk(u0 + CU, c0 + 1, u0, pair_of(c0 + 1), True, x_acts, k_all)
                with pe.Fori(1, 11) as i:
                    for c in range(2):
                        chunk(i * (2 * CU) + (u0 + CU * c), i * 2 + (c0 + c), u0, pair_of(c0 + c), True, x_acts, k_all)
                name = "ffn_out" + layer
                u0, c0 = UNIT0[name], CHUNK0[name]
                first_pair = 11 * "AB".index(layer)

                def wait_mid(u):
                    if u % 2 == 0:
                        pe.wait_ge(S.mid_lo_done, first_pair + u // 2 + 1)
                with pe.Fori(0, 2) as i:
                    for c in range(2):
                        chunk(i * (2 * FCU) + (u0 + FCU * c), i * 2 + (c0 + c), u0 + FCU * c, pair_of(c0 + c), False,
                              mid_acts, list(range(FKT)), before=wait_mid if c == 0 else None)

            ffn("A", 2)

            u0, c0 = UNIT0["qmB"], CHUNK0["qmB"]
            chunk(u0, c0, u0, pair_of(c0), True, x_acts, k_all, before=turns(3))
            spread_rstd(3)
            pe.wait_ge(S.xT_ready, TURN0[4])
            for c in range(9):
                def after(u, c=c):
                    n = CU * c + u
                    if n % 2 == 0 and 2 <= n <= 24:
                        mem_head(1, (n // 2 - 1) // 3, (n // 2 - 1) % 3)
                    if n in DIL_S:
                        dil_scores(DIL_S.index(n))
                    if n in DIL_PT:
                        dil_turn(DIL_PT.index(n))
                    if n in DIL_O:
                        dil_values(DIL_O.index(n))
                u0, c0 = UNIT0["kB"] + CU * c, CHUNK0["kB"] + c
                chunk(u0, c0, u0, pair_of(c0), c < 6, x_acts if 3 <= c < 6 else m_acts, k_all, after=after)

            def wait_mix_B(u):
                if u == 0:
                    pe.wait_ge(S.m_ready, 2 * HEADS_M)
                elif u >= 2:
                    pe.wait_ge(S.d_ready, GROUPS * -(-(2 * u - 2) // GROUPS))

            def last_trios(u):
                n = 9 * CU + u
                if n in DIL_O:
                    dil_values(DIL_O.index(n))

            for c in range(4):
                u0, c0 = UNIT0["outB"] + CU * c, CHUNK0["outB"] + c
                chunk(u0, c0, u0, pair_of(c0), False, mix_B, ORDER_B, before=wait_mix_B if c == 0 else None,
                      after=last_trios if c == 0 else None)
            ffn("B", 4)

        @block.scalar
        def _(act):
            def split(n, slot, first_use=False):
                act.wait_ge(landed[slot], n_landed(n, slot))
                if not first_use:
                    act.wait_ge(S.unit_used, n + (1 - RING))
                act.activation(w_hi[:, slot, :], raw[:, slot, :], ACT.Copy).then_inc(S.hi_done, 1)

            def n_landed(n, slot):
                if isinstance(n, int):
                    return 16 * (n // RING + 1)
                return n * 4 + (16 - 4 * slot)

            def split_range(n0, count):
                turns = count // RING if count > 2 * RING else 0
                if turns:
                    with act.Fori(0, turns) as i:
                        for u in range(RING):
                            split(i * RING + (n0 + u), (n0 + u) % RING)
                for n in range(n0 + turns * RING, n0 + count):
                    split(n, n % RING, n < RING)

            def norm_squares(n):
                src, _ = norm_plan(n)
                for t in range(TT):
                    if n + t:
                        act.wait_ge(S.sq_summed, TT * n + t)
                    if n == 0:
                        for q in range(4):
                            act.wait_ge(mem_in[q], 16)
                    elif n == 1:
                        act.wait_ge(S.x_in, 16)
                    else:
                        act.wait_ge(S.h_new, 4 * TT * (n - 1))
                    scraps, rows = ((small.rearrange("p (a b) -> p a b", a=4), src[:, :, t, :]) if n == 0 else
                                    (small, src[:, t, :]))
                    act.activation(scraps, rows, ACT.Square, accum_out=ssq(n)[:, t:t + 1]
                                   ).then_inc(S.sq_summed, 1)

            def norm_std(k):
                act.wait_ge(S.var_ready, k + 1)
                act.activation(st[:, 56:58], st[:, 54:56], ACT.Sqrt).then_inc(S.std_ready, 1)

            def load_sqrt():
                act.activation(scrap1, one, ACT.Sqrt)

            def x_rows(q):
                if q == 0:
                    act.wait_ge(S.rstd_ready, 1)
                if q >= 2:
                    act.wait_ge(S.tp_ready, GROUP0[1] + q - 1)
                for t in range(TT):
                    ins = act.activation(piece[:, q % 2, t * COLS:(t + 1) * COLS], h[:, t, q * COLS:(q + 1) * COLS],
                                         ACT.Copy, scale=rstd(1)[:, t:t + 1])
                ins.then_inc(S.hn_ready, 1)

            def turned_hi(n, q):
                _, targets = norm_plan(n)
                act.wait_ge(S.tp_ready, GROUP0[n] + q + 1)
                for row, hi_to, _ in targets:
                    for k in range(4):
                        ins = act.activation(hi_to[:, 4 * q + k, :], side_ps[q % 2][:, k * SEQ:(k + 1) * SEQ], ACT.Copy,
                                             scale=gain[:, row, 4 * q + k:4 * q + k + 1])
                ins.then_inc(S.xhi_ready, 1)

            def copy_spread(k):
                act.wait_ge(S.spread_done, k + 1)
                act.activation(spread[:], side_ps[0][:, 0:SEQ], ACT.Copy).then_inc(S.spread_ready, 1)

            def turned_chunk(n, k, u0):
                turned_hi(n, 0)
                turned_hi(n, 1)
                split_range(u0 + 4, 1)
                turned_hi(n, 2)
                split_range(u0 + 5, 2)
                turned_hi(n, 3)
                split_range(u0 + 7, 1)
                norm_squares(n)
                norm_std(k)

            def drain(c, dst):
                act.wait_ge(S.unit_used, units_by(c + 1))
                act.activation(dst, gemm_ps[c % 2][:], ACT.Copy).then_inc(S.chunk_drained, 1)

            def drain_values(c, dst, n):
                act.wait_ge(S.unit_used, units_by(c + 1))
                for t in range(TT):
                    ins = act.activation(dst[:, t, :], gemm_ps[c % 2][:, t * COLS:(t + 1) * COLS], ACT.Copy,
                                         scale=rstd(n)[:, t:t + 1])
                ins.then_inc(S.chunk_drained, 1)

            def y_squares(name, c):
                s = TOKEN_STAGES.index(name)
                act.wait_ge(S.sq_summed, (s + 2) * TT)
                act.wait_ge(S.chunk_drained, CHUNK0[name] + c)
                for t in range(TT):
                    act.wait_ge(S.y_scaled, TT * (4 * s + c) + t + 1)
                    ins = act.activation(token_buffers(name)[2][:, t * COLS:(t + 1) * COLS],
                                         gemm_ps[(CHUNK0[name] + c) % 2][:, t * COLS:(t + 1) * COLS],
                                         ACT.Square, accum_out=y_ssq(name)[:, 2 * c + t:2 * c + t + 1])
                ins.then_inc(S.chunk_drained, 1)

            def mem_softmax(layer, head):
                n = HEADS_M * layer + head
                act.wait_ge(S.att_mx, n + 1)
                for t in range(TT):
                    ins = act.activation(piece[:, 0, t * N_MEM:(t + 1) * N_MEM],
                                         side_ps[0][:, t * N_MEM:(t + 1) * N_MEM], ACT.Exp,
                                         bias=nmx[:, t:t + 1], scale=SCALE, accum_out=zz[:, t:t + 1])
                ins.then_inc(S.att_exp, 1)

            def mem_react(layer, slot):
                head, stp = slot // 3, slot % 3
                n = HEADS_M * layer + head
                if stp == 0:
                    mem_softmax(layer, head)
                elif stp == 1:
                    act.wait_ge(S.att_pt, n + 1)
                    act.activation(piece[:, 1, 0:COLS], side_ps[0][:, COLS:2 * COLS], ACT.Copy).then_inc(S.att_ptc, 1)
                else:
                    act.wait_ge(S.att_o, n + 1)
                    to = m_hi_B[:, head, :] if layer else mix_hi[:, HEADS_D + head, :]
                    act.activation(to, side_ps[0][:, 0:SEQ], ACT.Copy).then_inc(S.m_hi, 1)

            def gate_sigmoids(j, part):
                act.wait_ge(S.gates_done, 2 * j + part + 1)
                if part == 0 and j:
                    act.wait_ge(S.scan_done, j)
                for g, dst in enumerate((rr, ii)):
                    for b in range(2):
                        k = 2 * part + b
                        ins = act.activation(dst[:, k, :], side_ps[1][:, g * COLS + b * SEQ:g * COLS + (b + 1) * SEQ],
                                             ACT.Sigmoid, bias=lr[:, 5 + g, FT * j + k:FT * j + k + 1])
                ins.then_inc(S.gates_drained, 1)

            def decays(j):
                act.wait_ge(S.gates_drained, 2 * j + 2)
                if j == 0:
                    act.wait_ge(S.lru_c, 1)
                else:
                    act.wait_ge(S.scan_y, j)
                for b in range(FT):
                    k = FT * j + b
                    act.activation(bb[:, b, :], rr[:, b, :], ACT.Tanh, scale=lc[:, 1, k:k + 1])
                    ins = act.activation(aa[:, b, :], rr[:, b, :], ACT.Exp, scale=lc[:, 0, k:k + 1])
                ins.then_inc(S.decay_ready, 1)

            def root(j):
                act.wait_ge(S.ratio_ready, j + 1)
                act.activation(flat(rr[:]), flat(bb[:]), ACT.Sqrt, bias=tiny).then_inc(S.sqrt_done, 1)

            def y_hi_part(j):
                act.wait_ge(S.scan_y, j + 1)
                act.activation(flat(mix_hi[:, FT * j:FT * j + FT, :]), flat(ge[:]), ACT.Copy).then_inc(S.y_hi, 1)

            def copy_xb(j, c):
                act.wait_ge(S.unit_used, units_by(c + 1))
                if j:
                    act.wait_ge(S.conv_done, j)
                act.activation(xbp[:, :, TAPS - 1:], gemm_ps[c % 2][:].rearrange("p (a b) -> p a b", a=FT), ACT.Copy
                               ).then_inc(S.chunk_drained, 1)

            def gelu(j, c):
                act.wait_ge(S.unit_used, units_by(c + 1))
                if j:
                    act.wait_ge(S.y_ready, j)
                act.activation(flat(ge[:]), gemm_ps[c % 2][:], ACT.Gelu_apprx_tanh).then_inc(S.chunk_drained, 1)

            act.dma_start(ident[:], ident_in).then_inc(S.consts_in, 16)
            act.dma_start(flat(gain[:]), gains).then_inc(S.consts_in, 16)
            act.wait_ge(S.one_set, 1)
            load_sqrt()
            split_range(0, 4)
            act.wait_ge(S.consts_in, 32)
            turned_chunk(0, 0, 0)
            act.dma_start(h[:], x.rearrange("(t p) n -> p t n", p=P)).then_inc(S.x_in, 16)
            for n in range(CU, UNIT0["xg"]):
                split_range(n, 1)
                if n == 11:
                    copy_spread(0)
                    act.wait_ge(S.lru_abs, 1)
                    act.activation(lc[:, 2, :], lc[:, 2, :], ACT.Exp, scale=-1.0).then_inc(S.lru_ez, 1)
                if n == 12:
                    norm_squares(1)
                if n == 13:
                    norm_std(1)
                if n in (14, 16, 18, 20):
                    x_rows((n - 14) // 2)
                if n in (18, 20, 22, 24):
                    turned_hi(1, (n - 18) // 2)
                if n == 19:
                    drain_values(1, v_A, 0)
                if n == 35:
                    drain_values(3, v_B, 0)

            for n in range(7 * CU):
                split_range(UNIT0["xg"] + n, 1)
                if n == 3:
                    drain(CHUNK0["qmA"], flat(q_A[:]))
                if n % 2 == 0 and 6 <= n <= 28:
                    mem_react(0, n // 2 - 3)
                for c, (branch, j) in enumerate(XG):
                    if branch == "x" and n == LRU_AT[j]:
                        copy_xb(j, CHUNK0["xg"] + c)
                    if branch == "g" and n == CU * (c + 1) + 3:
                        gelu(j, CHUNK0["xg"] + c)
                for j, at_unit in enumerate(LRU_AT):
                    if n == at_unit + 5:
                        gate_sigmoids(j, 0)
                    if n == at_unit + 7:
                        gate_sigmoids(j, 1)
                    if n == at_unit + 8:
                        decays(j)
                    if n == at_unit + 10:
                        root(j)
                    if n == Y_AT[j]:
                        y_hi_part(j)

            def token_stage(name, units):
                for c in range(1, 4):
                    n0 = UNIT0[name] + units * c
                    split_range(n0, 4)
                    y_squares(name, c - 1)
                    split_range(n0 + 4, units - 4)

            def post_norm(name, k, norm, next_unit):
                split_range(next_unit, 4)
                load_sqrt()
                y_squares(name, 3)
                norm_std(k)
                turned_chunk(norm, k + 1, next_unit)

            def mid_hi_part(k, at_tile):
                act.wait_ge(S.hid_ready, k)
                act.activation(flat(mid_hi[:, at_tile, :]), piece[:, 1, :], ACT.Copy).then_inc(S.mid_hi_done, 1)

            def ffn_in(layer):
                name = "ffn_in" + layer
                u0 = UNIT0[name]
                k0 = 11 * "AB".index(layer)

                def one(i, first):
                    if not first:
                        for u in range(4):
                            split(i * 16 + (u0 + u), u)
                        mid_hi_part(i + k0, bass.ds(i * FT - FT, FT))
                        for u in range(4, 8):
                            split(i * 16 + (u0 + u), u % RING)
                    for u in range(8, 12):
                        split(i * 16 + (u0 + u), u % RING)
                    if first:
                        copy_spread(1 + 2 * "AB".index(layer))
                    act.wait_ge(S.chunk_drained, i * 2 + (CHUNK0[name] + 1))
                    act.activation(piece[:, 0, :], piece[:, 0, :], ACT.Silu).then_inc(S.silu_done, 1)
                    for u in range(12, 16):
                        split(i * 16 + (u0 + u), u % RING)
                one(0, True)
                with act.Fori(1, 11) as i:
                    one(i, False)
                n0 = UNIT0["ffn_out" + layer]
                split_range(n0, 4)
                mid_hi_part(k0 + 11, slice(FKT - FT, FKT))
                split_range(n0 + 4, FCU - 4)

            token_stage("outA", CU)
            post_norm("outA", 2, 2, UNIT0["ffn_inA"])
            ffn_in("A")
            token_stage("ffn_outA", FCU)
            post_norm("ffn_outA", 4, 3, UNIT0["qmB"])

            def dil_exp(i):
                act.wait_ge(S.dil_mx, i + 1)
                for t in range(TT):
                    ins = act.activation(dS[t], dS[t], ACT.Exp, bias=nmx[:, t:t + 1], scale=SCALE,
                                         accum_out=zz[:, t:t + 1])
                ins.then_inc(S.dil_exp, 1)

            for n in range(10 * CU):
                split_range(UNIT0["kB"] + n, 1)
                if n == 3:
                    copy_spread(2)
                if n % 2 == 0 and 6 <= n <= 28:
                    mem_react(1, n // 2 - 3)
                for c in range(3):
                    if n == CU * (7 + c) + 3:
                        drain_values(CHUNK0["vB"] + c, v_D[:, :, c * COLS:(c + 1) * COLS], 3)
                if n - 4 in DIL_S:
                    dil_exp(DIL_S.index(n - 4))
                if n - 4 in DIL_PT:
                    i = DIL_PT.index(n - 4)
                    for g in range(GROUPS):
                        act.wait_ge(S.dil_pt, GROUPS * i + g + 1)
                        act.activation(dPT[i][:, g * 384:(g + 1) * 384], dil_pt_ps(g), ACT.Copy).then_inc(S.dil_ptc, 1)
                if n - 4 in DIL_O:
                    i = DIL_O.index(n - 4)
                    for g in range(GROUPS):
                        act.wait_ge(S.dil_o, GROUPS * i + g + 1)
                        act.activation(d_hi[:, GROUPS * i + g, :], dil_o_ps(g), ACT.Copy).then_inc(S.d_hi, 1)
            token_stage("outB", CU)
            post_norm("outB", 6, 4, UNIT0["ffn_inB"])
            ffn_in("B")
            token_stage("ffn_outB", FCU)
            load_sqrt()
            y_squares("ffn_outB", 3)
            norm_std(8)

        @block.vector
        def _(dve):
            steps = [0]

            def step(ins):
                steps[0] += 1
                ins.then_inc(S.dve_step, 1)
                dve.wait_ge(S.dve_step, steps[0])

            def split(n, slot):
                dve.wait_ge(S.hi_done, n + 1)
                dve.tensor_tensor(w_lo[:, slot, :], raw[:, slot, :], w_hi[:, slot, :].bitcast(F32), ALU.subtract
                                  ).then_inc(S.lo_done, 1)

            def split_range(n0, count):
                turns = count // RING if count > 2 * RING else 0
                if turns:
                    with dve.Fori(0, turns) as i:
                        for u in range(RING):
                            split(i * RING + (n0 + u), (n0 + u) % RING)
                for n in range(n0 + turns * RING, n0 + count):
                    split(n, n % RING)

            def lo_part(dst, whole, hi):
                return dve.tensor_tensor(dst, whole, hi, ALU.subtract)

            def variance(src):
                dve.tensor_scalar(st[:, 54:56], src, 1.0 / D, EPS, ALU.mult, ALU.add).then_inc(S.var_ready, 1)

            def norm_var(n):
                dve.wait_ge(S.sq_summed, TT * (n + 1))
                variance(ssq(n))

            def norm_rstd(n, k):
                dve.wait_ge(S.std_ready, k + 1)
                dve.reciprocal(rstd(n), st[:, 56:58]).then_inc(S.rstd_ready, 1)

            def rstd_diag(n):
                for t in range(TT):
                    ins = dve.tensor_scalar(diag[:, t, :], ident[:], rstd(n)[:, t:t + 1], None, ALU.mult)
                ins.then_inc(S.diag_ready, 1)

            def turned_lo(n, q):
                _, targets = norm_plan(n)
                dve.wait_ge(S.xhi_ready, GROUP0[n] + q + 1)
                for row, hi_to, lo_to in targets:
                    for k in range(4):
                        ins = dve.scalar_tensor_tensor(lo_to[:, 4 * q + k, :], side_ps[q % 2][:, k * SEQ:(k + 1) * SEQ],
                                                       gain[:, row, 4 * q + k:4 * q + k + 1],
                                                       hi_to[:, 4 * q + k, :].bitcast(F32), ALU.mult, ALU.subtract)
                    ins.then_inc(S.xT_ready, 1)

            def turned_chunk(n, k, u0, h_rows=None):
                h_rows = h_rows or (lambda q: None)
                h_rows(0)
                h_rows(1)
                turned_lo(n, 0)
                h_rows(2)
                turned_lo(n, 1)
                h_rows(3)
                split_range(u0 + 4, 1)
                turned_lo(n, 2)
                split_range(u0 + 5, 2)
                turned_lo(n, 3)
                split_range(u0 + 7, 1)
                norm_var(n)
                dve.wait_ge(S.std_ready, k + 1)
                step(dve.reciprocal(rstd(n), st[:, 56:58]))
                rstd_diag(n)

            def drain(c, dst):
                k = 1 if c < CHUNK0["qmA"] else 3
                dve.wait_ge(S.spread_ready, k)
                dve.wait_ge(S.unit_used, units_by(c + 1))
                dve.tensor_tensor(dst, gemm_ps[c % 2][:].rearrange("p (a b) -> p a b", a=FT),
                                  spread[:].unsqueeze(1).to_broadcast([P, FT, SEQ]), ALU.mult
                                  ).then_inc(S.chunk_drained, 1)

            def y_scale(name, c):
                s = TOKEN_STAGES.index(name)
                cc = CHUNK0[name] + c
                y_to, g, _ = token_buffers(name)
                dve.wait_ge(S.unit_used, units_by(cc + 1))
                dve.wait_ge(S.post_g_in, 16 * (s + 1))
                cols = slice(c * COLS, (c + 1) * COLS)
                for t in range(TT):
                    dve.tensor_tensor(y_to[:, c, t, :], gemm_ps[cc % 2][:, t * COLS:(t + 1) * COLS], g[:, cols],
                                      ALU.mult).then_inc(S.y_scaled, 1)

            def y_norm(name, k):
                dve.wait_ge(S.chunk_drained, CHUNK0[name] + 4)
                step(dve.tensor_reduce(st[:, 42:44], y_ssq(name).rearrange("p (c t) -> p t c", t=TT), AX.X, ALU.add))
                variance(st[:, 42:44])
                dve.wait_ge(S.std_ready, k + 1)
                step(dve.reciprocal(y_rstd(), st[:, 56:58]))

            def residual(name, q):
                cols = slice(q * COLS, (q + 1) * COLS)
                for t in range(TT):
                    dve.scalar_tensor_tensor(h[:, t, cols], token_buffers(name)[0][:, q, t, :], y_rstd()[:, t:t + 1],
                                             h[:, t, cols], ALU.mult, ALU.add).then_inc(S.h_new, 1)

            def mem_react(layer, slot):
                head, stp = slot // 3, slot % 3
                n = HEADS_M * layer + head
                if stp == 0:
                    dve.wait_ge(S.att_s, n + 1)
                    step(dve.tensor_reduce(mx, side_ps[0][:, 0:COLS].rearrange("p (t n) -> p t n", t=TT), AX.X,
                                           ALU.max))
                    dve.tensor_scalar(nmx, mx, -SCALE, None, ALU.mult).then_inc(S.att_mx, 1)
                    dve.wait_ge(S.att_exp, n + 1)
                    step(dve.reciprocal(rz, zz))
                    for t in range(TT):
                        p = piece[:, 0, t * N_MEM:(t + 1) * N_MEM]
                        ins = dve.tensor_scalar(p, p, rz[:, t:t + 1], None, ALU.mult)
                    ins.then_inc(S.att_p, 1)
                elif stp == 2:
                    dve.wait_ge(S.m_hi, n + 1)
                    to, hi = ((m_lo_B[:, head, :], m_hi_B[:, head, :]) if layer else
                              (mix_lo[:, HEADS_D + head, :], mix_hi[:, HEADS_D + head, :]))
                    lo_part(to, side_ps[0][:, 0:SEQ], hi.bitcast(F32)).then_inc(S.m_ready, 1)

            def conv(j, k):
                if k == TAPS - 1:
                    c = CHUNK0["xg"] + XG.index(("x", j))
                    dve.wait_ge(S.chunk_drained, c + 1)
                    if j == 0:
                        dve.wait_ge(S.pads_zero, 1)
                else:
                    dve.wait_ge(S.tap_done, (TAPS - 1) * j + TAPS - 1 - k)
                for b in range(FT):
                    n = FT * j + b
                    w = lr[:, k, n:n + 1]
                    src = xbp[:, b, k:k + SEQ]
                    if k == TAPS - 1:
                        ins = dve.tensor_scalar(xc[:, b, :], src, w, lr[:, 4, n:n + 1], ALU.mult, ALU.add)
                    else:
                        ins = dve.scalar_tensor_tensor(xc[:, b, :], src, w, xc[:, b, :], ALU.mult, ALU.add)
                ins.then_inc(S.tap_done if k else S.conv_done, 1)

            def lru_input(j):
                dve.wait_ge(S.gates_drained, 2 * j + 2)
                step(dve.tensor_tensor(flat(ii[:]), flat(ii[:]), flat(xc[:]), ALU.mult))

            def lru_ratio(j):
                dve.wait_ge(S.decay_ready, j + 1)
                step(dve.tensor_tensor(flat(rr[:]), flat(aa[:]), flat(aa[:]), ALU.mult))
                dve.scalar_tensor_tensor(flat(bb[:]), flat(rr[:]), 1.0, flat(bb[:]), ALU.add, ALU.mult
                                         ).then_inc(S.ratio_ready, 1)

            def lru_scan(j):
                dve.wait_ge(S.sqrt_done, j + 1)
                step(dve.tensor_tensor(flat(bb[:]), flat(rr[:]), flat(ii[:]), ALU.mult))
                for b in range(FT):
                    ins = dve.tensor_tensor_scan(bb[:, b, :], aa[:, b, :], bb[:, b, :], 0.0, ALU.mult, ALU.add)
                ins.then_inc(S.scan_done, 1)

            def lru_out(j):
                dve.wait_ge(S.scan_done, j + 1)
                dve.wait_ge(S.chunk_drained, CHUNK0["xg"] + XG.index(("g", j)) + 1)
                dve.tensor_tensor(flat(ge[:]), flat(bb[:]), flat(ge[:]), ALU.mult).then_inc(S.scan_y, 1)
                dve.wait_ge(S.y_hi, j + 1)
                lo_part(flat(mix_lo[:, FT * j:FT * j + FT, :]), flat(ge[:]),
                        flat(mix_hi[:, FT * j:FT * j + FT, :]).bitcast(F32)).then_inc(S.y_ready, 1)

            def decay_constants():
                lam, z, s, s2, acc, t = (lr[:, 7, :], lc[:, 2, :], lc[:, 3, :], lc[:, 4, :], lc[:, 5, :], lc[:, 6, :])
                dve.wait_ge(S.lru_ez, 1)
                step(dve.tensor_scalar(t, z, 2.0, None, ALU.add))
                step(dve.reciprocal(t, t))
                step(dve.tensor_tensor(s, z, t, ALU.mult))
                step(dve.tensor_tensor(s2, s, s, ALU.mult))
                top = 17
                step(dve.tensor_scalar(acc, s2, 1.0 / top, 1.0 / (top - 2), ALU.mult, ALU.add))
                for k in range(top - 4, 0, -2):
                    step(dve.tensor_tensor(acc, acc, s2, ALU.mult))
                    step(dve.tensor_scalar(acc, acc, 1.0 / k, None, ALU.add))
                step(dve.tensor_tensor(acc, acc, s, ALU.mult))
                step(dve.tensor_scalar(t, lam, -1.0, 0.0, ALU.mult, ALU.max))
                step(dve.scalar_tensor_tensor(t, acc, 2.0, t, ALU.mult, ALU.add))
                step(dve.tensor_scalar(lc[:, 0, :], t, -LRU_C, None, ALU.mult))
                dve.tensor_scalar(lc[:, 1, :], t, LRU_C, None, ALU.mult).then_inc(S.lru_c, 1)

            dve.memset(one, 1.0)
            dve.memset(tiny, 1e-30).then_inc(S.one_set, 1)
            split_range(0, 4)
            dve.wait_ge(S.consts_in, 32)
            turned_chunk(0, 0, 0)
            dve.wait_ge(S.lru_in, 16)
            lam = lr[:, 7, :]
            step(dve.tensor_scalar(lc[:, 7, :], lam, -1.0, None, ALU.mult))
            dve.tensor_tensor(lc[:, 2, :], lc[:, 7, :], lam, ALU.max).then_inc(S.lru_abs, 1)
            for n in range(CU, UNIT0["xg"]):
                split_range(n, 1)
                if n == 11:
                    drain(0, kT_A[:])
                if n == 12:
                    norm_var(1)
                if n == 13:
                    norm_rstd(1, 1)
                if n in (18, 20, 22, 24):
                    turned_lo(1, (n - 18) // 2)
                if n == 27:
                    drain(2, kT_B)
                if n == 30:
                    decay_constants()

            for n in range(7 * CU):
                split_range(UNIT0["xg"] + n, 1)
                if n % 2 == 0 and 6 <= n <= 28:
                    mem_react(0, n // 2 - 3)
                for j, at_unit in enumerate(LRU_AT):
                    if at_unit <= n < at_unit + TAPS:
                        conv(j, TAPS - 1 - (n - at_unit))
                    if n == at_unit + 8:
                        lru_input(j)
                    if n == at_unit + 9:
                        lru_ratio(j)
                    if n == at_unit + 11:
                        lru_scan(j)
                    if n == Y_AT[j]:
                        lru_out(j)

            def token_stage(name, units):
                for c in range(1, 4):
                    n0 = UNIT0[name] + units * c
                    split_range(n0, 4)
                    y_scale(name, c - 1)
                    split_range(n0 + 4, units - 4)

            def post_norm(name, k, norm, next_unit):
                split_range(next_unit, 4)
                y_scale(name, 3)
                y_norm(name, k)
                turned_chunk(norm, k + 1, next_unit, lambda q: residual(name, q))

            def ffn_in(layer):
                name = "ffn_in" + layer
                u0, c0 = UNIT0[name], CHUNK0[name]
                k0 = 11 * "AB".index(layer)

                def scaled(to, c, u):
                    dve.wait_ge(S.unit_used, u)
                    dve.tensor_tensor(piece[:, to, :].rearrange("p (a b) -> p a b", a=FT),
                                      gemm_ps[(c0 + to) % 2][:].rearrange("p (a b) -> p a b", a=FT),
                                      spread[:].unsqueeze(1).to_broadcast([P, FT, SEQ]), ALU.mult
                                      ).then_inc(S.chunk_drained, 1)

                def hidden(k, c, u, at_tile):
                    if not isinstance(k, int) or k > 1:
                        dve.wait_ge(S.mid_lo_done, k - 1)
                    scaled(1, c, u)
                    dve.wait_ge(S.chunk_drained, c)
                    dve.wait_ge(S.silu_done, k)
                    dve.tensor_tensor(piece[:, 1, :], piece[:, 1, :], piece[:, 0, :], ALU.mult).then_inc(S.hid_ready, 1)
                    dve.wait_ge(S.mid_hi_done, k)
                    lo_part(flat(mid_lo[:, at_tile, :]), piece[:, 1, :], flat(mid_hi[:, at_tile, :]).bitcast(F32)
                            ).then_inc(S.mid_lo_done, 1)

                def one(i, first):
                    if not first:
                        for u in range(4):
                            split(i * 16 + (u0 + u), u)
                        hidden(i + k0, i * 2 + c0, i * 16 + u0,
                               slice(0, FT) if isinstance(i, int) else bass.ds(i * FT - FT, FT))
                        for u in range(4, 8):
                            split(i * 16 + (u0 + u), u % RING)
                    for u in range(8, 12):
                        split(i * 16 + (u0 + u), u % RING)
                    if first:
                        dve.wait_ge(S.spread_ready, (2, 4)["AB".index(layer)])
                    scaled(0, i * 2 + c0, i * 16 + (u0 + CU))
                    for u in range(12, 16):
                        split(i * 16 + (u0 + u), u % RING)
                one(0, True)
                one(1, False)
                with dve.Fori(2, 11) as i:
                    one(i, False)
                n0 = UNIT0["ffn_out" + layer]
                split_range(n0, 4)
                hidden(k0 + 11, c0 + 22, n0, slice(FKT - FT, FKT))
                split_range(n0 + 4, FCU - 4)

            token_stage("outA", CU)
            post_norm("outA", 2, 2, UNIT0["ffn_inA"])
            ffn_in("A")
            token_stage("ffn_outA", FCU)
            post_norm("ffn_outA", 4, 3, UNIT0["qmB"])

            def dil_softmax(i):
                dve.wait_ge(S.dil_s, i + 1)
                if i == 0:
                    dve.wait_ge(S.far_in, 16)
                else:
                    dve.wait_ge(S.dil_pt, GROUPS * i)
                for g in range(GROUPS):
                    slope = -(2.0 ** (-8.0 * (PER_GROUP * g + i + 1) / HEADS_D)) / SCALE
                    ps0, ps1 = dil_scores_ps(g)
                    dve.scalar_tensor_tensor(dS[0][:, g * P:(g + 1) * P], far[:, g, P:2 * P], slope, ps0, ALU.mult,
                                             ALU.add)
                    ins = dve.scalar_tensor_tensor(dS[1][:, g * SEQ:(g + 1) * SEQ], far[:, g, :], slope, ps1, ALU.mult,
                                                   ALU.add)
                step(ins)
                dve.tensor_reduce(mx[:, 0:1], dS[0], AX.X, ALU.max)
                step(dve.tensor_reduce(mx[:, 1:2], dS[1], AX.X, ALU.max))
                dve.tensor_scalar(nmx, mx, -SCALE, None, ALU.mult).then_inc(S.dil_mx, 1)
                dve.wait_ge(S.dil_exp, i + 1)
                step(dve.reciprocal(rz, zz))
                for t in range(TT):
                    ins = dve.tensor_scalar(dS[t], dS[t], rz[:, t:t + 1], None, ALU.mult)
                ins.then_inc(S.dil_p, 1)

            for n in range(10 * CU):
                split_range(UNIT0["kB"] + n, 1)
                if n == 3:
                    drain(CHUNK0["qmB"], q_B[:])
                if n % 2 == 0 and 6 <= n <= 28:
                    mem_react(1, n // 2 - 3)
                for c in range(3):
                    if n == CU * (1 + c) + 3:
                        drain(CHUNK0["kB"] + c, kT_D[:, FT * c:FT * c + FT, :])
                    if n == CU * (4 + c) + 3:
                        drain(CHUNK0["qB"] + c, q_D[:, FT * c:FT * c + FT, :])
                if n - 4 in DIL_S:
                    dil_softmax(DIL_S.index(n - 4))
                if n - 4 in DIL_O:
                    i = DIL_O.index(n - 4)
                    for g in range(GROUPS):
                        dve.wait_ge(S.d_hi, GROUPS * i + g + 1)
                        lo_part(d_lo[:, GROUPS * i + g, :], dil_o_ps(g), d_hi[:, GROUPS * i + g, :].bitcast(F32)
                                ).then_inc(S.d_ready, 1)
            token_stage("outB", CU)
            post_norm("outB", 6, 4, UNIT0["ffn_inB"])
            ffn_in("B")
            token_stage("ffn_outB", FCU)
            y_scale("ffn_outB", 3)
            y_norm("ffn_outB", 8)
            for q in range(4):
                residual("ffn_outB", q)


def tiles(w, k_order, cols):
    out = []
    for c in cols:
        block = w[:, c:c + COLS].reshape(-1, P, COLS)[k_order]
        block = block.reshape(-1, UK, P, COLS).transpose(0, 2, 1, 3)
        out.append(block.reshape(-1, P, UNIT))
    return out


def by_trio(w):
    return w.reshape(len(w), HEADS_D, P)[:, TRIO_HEADS].reshape(len(w), -1)


def by_partition(v):
    return v.reshape(-1, P).T


def kernel(**inputs):
    import concourse.bacc as bacc
    from concourse.bass_utils import run_bass_kernel_spmd

    a = {k: np.asarray(v) for k, v in inputs.items()}
    d_all, f_all = list(range(KT)), list(range(FKT))
    units = []
    units += tiles(a["a_w_mem_kv"][0], d_all, (0, 512))
    units += tiles(a["b_w_mem_kv"][0], d_all, (0, 512))
    units += tiles(a["a_w_in"][0], d_all, (3072, *(512 * j + (1536 if branch == "g" else 0) for branch, j in XG)))
    units += tiles(a["a_w_out"][0], ORDER_A, range(0, D, COLS))
    pairs = [c for j in range(0, D_FF, COLS) for c in (j, D_FF + j)]
    units += tiles(a["a_w_ffn_in"][0], d_all, pairs)
    units += tiles(a["a_w_ffn_out"][0], f_all, range(0, D, COLS))
    units += tiles(a["b_w_in"][0], d_all, (1536,))
    units += tiles(a["w_kv_shared"], d_all, (0, 512, 1024))
    units += tiles(by_trio(a["b_w_in"][0][:, :HEADS_D * P]), d_all, (0, 512, 1024))
    units += tiles(by_trio(a["w_kv_shared"][:, HEADS_D * P:]), d_all, (0, 512, 1024))
    units += tiles(a["b_w_out"][0], ORDER_B, range(0, D, COLS))
    units += tiles(a["b_w_ffn_in"][0], d_all, pairs)
    units += tiles(a["b_w_ffn_out"][0], f_all, range(0, D, COLS))
    stream = np.concatenate(units)

    gains = np.concatenate([by_partition(v) for v in (
        a["mem_norm_g"], a["a_pre_mix_g"][0], a["a_pre_ffn_g"][0], a["kv_norm_g"], a["b_pre_mix_g"][0],
        a["b_pre_ffn_g"][0])], axis=1)
    lru = np.concatenate([by_partition(v) for v in (
        *a["a_conv_w"][0], a["a_conv_b"][0], a["a_gate_a_b"][0], a["a_gate_x_b"][0], a["a_lambda"][0])], axis=1)
    gate_w = np.concatenate([a["a_gate_a_w"][0], a["a_gate_x_w"][0]]).transpose(1, 0, 2).reshape(P, -1)
    post_g = np.stack([a["a_post_mix_g"][0], a["a_post_ffn_g"][0], a["b_post_mix_g"][0], a["b_post_ffn_g"][0]])

    rel = np.arange(P)[:, None] + P - np.arange(2 * P)[None, :]
    dist = np.stack([np.where((rel >= 0) & (rel % d == 0) & ((rel <= P) if d == 1 else True), rel, FAR)
                     for d in DIL], axis=1).reshape(P, -1).astype(np.float32)
    arrays = {"stream": stream, "x": a["x"][0], "mem": a["mem"][0], "gains": gains, "lru": lru, "gate_w": gate_w,
              "post_g": post_g, "dist": dist, "ident": np.eye(P, dtype=np.float32)}
    arrays = {k: np.ascontiguousarray(v) for k, v in arrays.items()}

    nc = bacc.Bacc("TRN2", target_bir_lowering=False, num_devices=1)
    args = [nc.dram_tensor(k, v.shape, mybir.dt.from_np(v.dtype), kind="ExternalInput").ap() for k, v in arrays.items()]
    args.append(nc.dram_tensor("out", (SEQ, D), F32, kind="ExternalOutput").ap())
    build(nc, *args)
    r = run_bass_kernel_spmd(nc, [arrays], core_ids=[0])
    return r.results[0]["out"].reshape(1, SEQ, D)
```

```python
from contextlib import ExitStack

import concourse.bass as bass
import numpy as np
from concourse import mybir

F32 = mybir.dt.float32
F32R = mybir.dt.float32r
ALU = mybir.AluOpType
ACT = mybir.ActivationFunctionType
AX = mybir.AxisListType

P = 128
D = 2048
SEQ = 256
N_MEM = 256
TT = SEQ // P
KT = D // P
HEADS_M = 4
HEADS_D = 12
LRU_BLOCKS = 12
TAPS = 4
D_FF = 5632
FKT = D_FF // P
COLS = 512
FT = COLS // P
UK = 2
UNIT = UK * COLS
RING = 4
CU = KT // UK
FCU = FKT // UK
EPS = 1e-6
SCALE = float(P) ** -0.5
LRU_C = 8.0
DIL = (1, 4, 16)
GROUPS = len(DIL)
PER_GROUP = HEADS_D // GROUPS
FAR = 1e30

ORDER_A = [12, 13, 14, 15] + list(range(12))
TRIO_HEADS = [PER_GROUP * g + i for i in range(PER_GROUP) for g in range(GROUPS)]
ORDER_B = [12, 13, 14, 15] + TRIO_HEADS

DIL_S, DIL_PT, DIL_O = (33, 41, 49, 57), (37, 45, 53, 61), (66, 69, 73, 74)

XG = (("x", 0), ("g", 0), ("x", 1), ("x", 2), ("g", 1), ("g", 2))
LRU_AT = (12, 27, 39)
Y_AT = (33, 45, 53)

STAGES = (("memA", 2, CU), ("memB", 2, CU), ("qmA", 1, CU), ("xg", 6, CU), ("outA", 4, CU),
          ("ffn_inA", 22, CU), ("ffn_outA", 4, FCU), ("qmB", 1, CU), ("kB", 3, CU), ("qB", 3, CU), ("vB", 3, CU),
          ("outB", 4, CU), ("ffn_inB", 22, CU), ("ffn_outB", 4, FCU))
UNIT0, CHUNK0 = {}, {}
_u = _c = 0
for _name, _chunks, _units in STAGES:
    UNIT0[_name], CHUNK0[_name] = _u, _c
    _u += _chunks * _units
    _c += _chunks
N_UNITS = _u


class Sems:

    def __init__(self, sem):
        self.consts_in = sem("consts_in")
        self.gates_in = sem("gates_in")
        self.lru_in = sem("lru_in")
        self.x_in = sem("x_in")
        self.post_g_in = sem("post_g_in")
        self.out_stored = sem("out_stored")
        self.hi_done = sem("hi_done")
        self.lo_done = sem("lo_done")
        self.unit_used = sem("unit_used")
        self.tile0_done = sem("tile0_done")
        self.chunk_drained = sem("chunk_drained")
        self.y_squared = sem("y_squared")
        self.sq_summed = sem("sq_summed")
        self.var_ready = sem("var_ready")
        self.std_ready = sem("std_ready")
        self.rstd_ready = sem("rstd_ready")
        self.diag_ready = sem("diag_ready")
        self.spread_done = sem("spread_done")
        self.spread_ready = sem("spread_ready")
        self.h_new = sem("h_new")
        self.hn_ready = sem("hn_ready")
        self.tp_ready = sem("tp_ready")
        self.xhi_ready = sem("xhi_ready")
        self.xT_ready = sem("xT_ready")
        self.pads_zero = sem("pads_zero")
        self.ones_set = sem("ones_set")
        self.tap_done = sem("tap_done")
        self.one_set = sem("one_set")
        self.lru_abs = sem("lru_abs")
        self.lru_ez = sem("lru_ez")
        self.lru_c = sem("lru_c")
        self.conv_done = sem("conv_done")
        self.gates_done = sem("gates_done")
        self.gates_drained = sem("gates_drained")
        self.decay_ready = sem("decay_ready")
        self.ratio_ready = sem("ratio_ready")
        self.sqrt_done = sem("sqrt_done")
        self.scan_done = sem("scan_done")
        self.scan_y = sem("scan_y")
        self.y_hi = sem("y_hi")
        self.y_ready = sem("y_ready")
        self.mid_hi_done = sem("mid_hi_done")
        self.silu_done = sem("silu_done")
        self.hid_ready = sem("hid_ready")
        self.mid_lo_done = sem("mid_lo_done")
        self.att_s = sem("att_s")
        self.att_mx = sem("att_mx")
        self.att_exp = sem("att_exp")
        self.att_p = sem("att_p")
        self.att_pt = sem("att_pt")
        self.att_ptc = sem("att_ptc")
        self.att_o = sem("att_o")
        self.m_hi = sem("m_hi")
        self.m_ready = sem("m_ready")
        self.dil_s = sem("dil_s")
        self.dil_mx = sem("dil_mx")
        self.dil_exp = sem("dil_exp")
        self.dil_p = sem("dil_p")
        self.dil_pt = sem("dil_pt")
        self.dil_ptc = sem("dil_ptc")
        self.dil_o = sem("dil_o")
        self.d_hi = sem("d_hi")
        self.d_ready = sem("d_ready")
        self.dve_step = sem("dve_step")
        self.far_in = sem("far_in")


def units_by(c):
    for name, chunks, units in STAGES:
        if c <= CHUNK0[name] + chunks:
            return UNIT0[name] + units * (c - CHUNK0[name])

NORM_GAINS = (1, 1, 1, 2, 1)
GROUPS_N = KT // UK
GROUP0 = [GROUPS_N * n for n in range(5)]
TURN0 = [GROUPS_N * sum(NORM_GAINS[:n]) for n in range(5)]
TOKEN_STAGES = ("outA", "ffn_outA", "outB", "ffn_outB")


def build(nc, stream, x, mem, gains, lru, gate_w, post_g, dist, ident_in, out):
    with ExitStack() as ctx:
        def sb(name, shape, dt=F32):
            return ctx.enter_context(nc.sbuf_tensor(name, shape, dt))

        S = Sems(lambda name: ctx.enter_context(nc.semaphore(name)))
        landed = [ctx.enter_context(nc.semaphore(f"landed{s}")) for s in range(RING)]

        raw = sb("raw", [P, RING, UNIT])
        w_hi = sb("w_hi", [P, RING, UNIT], F32R)
        w_lo = sb("w_lo", [P, RING, UNIT], F32R)
        h = sb("h", [P, TT, D])
        piece = sb("piece", [P, 2, TT * COLS])
        kv_B = sb("kv_B", [P, 2, HEADS_M * N_MEM])
        ident = sb("identity", [P, P])
        ones = sb("ones", [P, P])
        diag = sb("diag", [P, TT, P])
        spread = sb("spread", [P, SEQ])
        gain = sb("gain", [P, 6, KT])
        lr = sb("lr", [P, 8, LRU_BLOCKS])
        lc = sb("lc", [P, 8, LRU_BLOCKS])
        st = sb("st", [P, 64])

        x_size, m_size = 2 * KT * SEQ * 4, 2 * FKT * SEQ * 4
        x_at = (nc.sbuf_base + 31) // 32 * 32
        sb("area", [P, (x_size + m_size) // 4])
        m_at = x_at + x_size

        def at(name, shape, offset, dt=F32):
            return nc.alloc_sbuf_tensor_at(name, shape, dt, offset=offset)

        half = KT * SEQ * 4
        xT_hi = at("xT_hi", [P, KT, SEQ], x_at, F32R)
        xT_lo = at("xT_lo", [P, KT, SEQ], x_at + half, F32R)
        mem_rows = at("mem_rows", [P, 4, TT, COLS], x_at)
        yg = at("yg", [P, GROUPS_N, TT, UK * P], x_at)
        pg = at("pg", [P, D], x_at + 16384)
        scrap = at("scrap", [P, D], x_at + 24576)
        d_hi = at("d_hi", [P, HEADS_D, SEQ], x_at, F32R)
        d_lo = at("d_lo", [P, HEADS_D, SEQ], x_at + 12288, F32R)
        mix_hi = at("mix_hi", [P, KT, SEQ], m_at, F32R)
        mix_lo = at("mix_lo", [P, KT, SEQ], m_at + half, F32R)
        o = m_at + 2 * half
        kT_A = at("kT_A", [P, HEADS_M, N_MEM], o)
        v_A = at("v_A", [P, 2, COLS], o + 4096)
        q_A = at("q_A", [P, HEADS_M, SEQ], o + 8192)
        gw = at("gw", [P, 2 * LRU_BLOCKS, P], o + 12288)
        xbp = at("xbp", [P, FT, SEQ + TAPS - 1], o + 24576)
        o2 = o + 24576 + 4352
        xc, rr, ii, aa, bb, ge = (at(n, [P, FT, SEQ], o2 + 4096 * k)
                                  for k, n in enumerate(("xc", "rr", "ii", "aa", "bb", "ge")))
        kT_D = at("kT_D", [P, HEADS_D, SEQ], o)
        v_D = at("v_D", [P, TT, HEADS_D * P], o + 12288)
        q_D = at("q_D", [P, HEADS_D, SEQ], o + 24576)
        far = at("far", [P, GROUPS, 2 * P], o + 36864)
        m_hi_B = at("m_hi_B", [P, HEADS_M, SEQ], o + 43008, F32R)
        m_lo_B = at("m_lo_B", [P, HEADS_M, SEQ], o + 47104, F32R)
        q_B = at("q_B", [P, HEADS_M, SEQ], o + 51200)
        yg_B = at("yg_B", [P, GROUPS_N, TT, UK * P], m_at)
        pg_B = at("pg_B", [P, D], m_at + 16384)
        scrap_B = at("scrap_B", [P, D], m_at + 24576)
        kT_B, v_B = kv_B[:, 0, :].rearrange("p (a b) -> p a b", a=HEADS_M), kv_B[:, 1, :].rearrange(
            "p (a b) -> p a b", a=2)
        kv_flat = kv_B[:].rearrange("p a b -> p (a b)")
        small = piece[:].rearrange("p a b -> p (a b)")
        dS = (kv_flat[:, 1152:1536], small[:, 1152:1920])
        dPT = (small[:, 0:1152], kv_flat[:, 0:1152], at("dPT2", [P, 1152], o + 51200)[:],
               at("dPT3", [P, 1152], x_at + 24576)[:])
        mid_hi = at("mid_hi", [P, FKT, SEQ], m_at, F32R)
        mid_lo = at("mid_lo", [P, FKT, SEQ], m_at + FKT * SEQ * 4, F32R)

        gemm_ps = [ctx.enter_context(nc.psum_tensor(f"gemm_ps{i}", [P, 1024], F32)) for i in range(2)]
        side_ps = [ctx.enter_context(nc.psum_tensor(f"side_ps{i}", [P, 1024], F32)) for i in range(2)]

        block = ctx.enter_context(nc.Block())

        def norm_plan(n):
            to_x, to_m = (xT_hi, xT_lo), (mix_hi, mix_lo)
            return ((mem_rows, ((0, *to_m),)), (h, ((1, *to_x),)), (h, ((2, *to_x),)),
                    (h, ((4, *to_x), (3, *to_m))), (h, ((5, *to_x),)))[n]

        def turned_ps(g):
            return side_ps[g // 2 % 2][:, g % 2 * COLS:(g % 2 + 1) * COLS]

        def token_buffers(name):
            return (yg_B, pg_B, scrap_B) if name == "outB" else (yg, pg, scrap)

        def ssq(n):
            return st[:, 2 * n:2 * n + 2]

        def rstd(n):
            return st[:, 10 + 2 * n:12 + 2 * n]

        def y_ssq(name):
            return st[:, 32:40]

        def y_rstd():
            return st[:, 40:42]

        mx, nmx, zz, rz = st[:, 44:46], st[:, 46:48], st[:, 48:50], st[:, 50:52]
        tiny, one, scrap1 = st[:, 60:61], st[:, 61:62], st[:, 62:63]
        mem_in = [ctx.enter_context(nc.semaphore(f"mem_in{q}")) for q in range(4)]

        def flat(ap):
            return ap.rearrange("p a b -> p (a b)")

        def head_slot(head):
            return TRIO_HEADS.index(head)

        def dil_scores_ps(g):
            return side_ps[1][:, g * P:(g + 1) * P], side_ps[0][:, g * SEQ:(g + 1) * SEQ]

        def dil_pt_ps(g):
            return (side_ps[1][:, 512:896], side_ps[0][:, 0:384], side_ps[1][:, 0:384])[g]

        def dil_o_ps(g):
            return (side_ps[0][:, 768:1024], side_ps[0][:, 0:256], side_ps[1][:, 0:256])[g]

        @block.sync
        def _(sp):
            def load_mem(q):
                cols = slice(q * COLS, (q + 1) * COLS)
                sp.dma_start(mem_rows[:, q, :, :], mem[:, cols].rearrange("(t p) n -> p t n", p=P)
                             ).then_inc(mem_in[q], 16)

            def load_unit(s):
                sp.dma_start(raw[:, s, :], stream[s]).then_inc(landed[s], 16)

            load_mem(0)
            load_unit(0)
            load_mem(1)
            load_unit(1)
            load_unit(2)
            load_mem(2)
            load_unit(3)
            load_mem(3)
            with sp.Fori(1, N_UNITS // RING) as i:
                for s in range(RING):
                    sp.wait_ge(S.lo_done, i * RING + (s + 1 - RING))
                    sp.dma_start(raw[:, s, :], stream[bass.ds(i * RING + s, 1)].rearrange("a p n -> (a p) n")
                                 ).then_inc(landed[s], 16)
            for q in range(4):
                cols = slice(q * COLS, (q + 1) * COLS)
                sp.wait_ge(S.h_new, 3 * GROUPS_N * TT + TT * (q + 1))
                sp.dma_start(out[:, cols].rearrange("(t p) n -> p t n", p=P), h[:, :, cols]).then_inc(S.out_stored, 16)
            sp.wait_ge(S.out_stored, 16 * 4)

        @block.gpsimd
        def _(pool):
            pool.memset(ones[:], 1.0).then_inc(S.ones_set, 1)
            pool.dma_start(flat(lr[:]), lru).then_inc(S.lru_in, 16)
            pool.memset(xbp[:, :, 0:TAPS - 1], 0.0).then_inc(S.pads_zero, 1)
            for g in range(2):
                pool.wait_ge(S.unit_used, CU * (2 + g))
                n = LRU_BLOCKS * P
                pool.dma_start(flat(gw[:])[:, g * n:(g + 1) * n], gate_w[:, g * n:(g + 1) * n]
                               ).then_inc(S.gates_in, 16)
            for n, name in enumerate(TOKEN_STAGES):
                pool.wait_ge(S.unit_used, UNIT0[name])
                pool.dma_start(token_buffers(name)[1][:], post_g[n:n + 1, :].to_broadcast([P, D])
                               ).then_inc(S.post_g_in, 16)
                if name == "ffn_outA":
                    pool.wait_ge(S.unit_used, UNIT0["qmB"])
                    pool.dma_start(flat(far[:]), dist).then_inc(S.far_in, 16)

        @block.tensor
        def _(pe):
            def unit(n, slot, feature, acts, kts, first, last, pair, tiles):
                acc = gemm_ps[pair]
                pe.wait_ge(S.lo_done, n + 1)
                for k, kt in enumerate(kts):
                    a_hi, a_lo = acts(kt)
                    for t in tiles:
                        w = slice(k * COLS + (t * P if feature else 0), k * COLS + (t * P + P if feature else COLS))
                        for part, (w_part, a_part) in enumerate(((w_hi, a_hi), (w_hi, a_lo), (w_lo, a_hi))):
                            begin = first and k == 0 and part == 0
                            end = last and k == UK - 1 and part == 2
                            if feature:
                                mm = pe.matmul(acc[:, t * SEQ:(t + 1) * SEQ], w_part[:, slot, w], a_part,
                                               start=begin and t % 2 == 0, stop=end, skip_group_check=True)
                            else:
                                mm = pe.matmul(acc[:, t * COLS:(t + 1) * COLS], a_part[:, t * P:(t + 1) * P],
                                               w_part[:, slot, w], start=begin, stop=end)
                return mm

            def chunk(n, c, base, pair, feature, acts, kts, before=None, after=None, tile0_first=False):
                if not isinstance(c, int) or c >= 2:
                    pe.wait_ge(S.chunk_drained, c - 1)
                units = len(kts) // UK

                def products(u, tiles):
                    return unit(n + u, (base + u) % RING, feature, acts, kts[UK * u:UK * u + UK], u == 0,
                                u == units - 1, pair, tiles)
                for u in range(units - 2 if tile0_first else units):
                    if before:
                        before(u)
                    products(u, range(FT if feature else TT)).then_inc(S.unit_used, 1)
                    if after:
                        after(u)
                if tile0_first:
                    if before:
                        before(units - 2)
                        before(units - 1)
                    products(units - 2, [0])
                    products(units - 1, [0]).then_inc(S.tile0_done, 1)
                    products(units - 2, [1]).then_inc(S.unit_used, 1)
                    products(units - 1, [1]).then_inc(S.unit_used, 1)

            def turn_group(n, g):
                src, _ = norm_plan(n)
                if n == 0:
                    if g == 0:
                        pe.wait_ge(S.consts_in, 32)
                    pe.wait_ge(mem_in[g // 2], 16)
                elif n == 1:
                    pe.wait_ge(S.hn_ready, g // 2 + 1)
                    if g == 0:
                        pe.wait_ge(S.spread_ready, 1)
                else:
                    pe.wait_ge(S.h_new, TT * (GROUPS_N * (n - 2) + g + 1))
                if GROUP0[n] + g >= 4:
                    m, gg = (n, g - 4) if g >= 4 else (n - 1, g + 4)
                    pe.wait_ge(S.xT_ready, TURN0[m] + NORM_GAINS[m] * (gg + 1))
                for k in range(UK):
                    for t in range(TT):
                        col = (UK * (g % 2) + k) * P
                        rows = (piece[:, g // 2 % 2, t * COLS + col:t * COLS + col + P] if n == 1 else
                                src[:, g // 2, t, col:col + P] if n == 0 else
                                src[:, t, (UK * g + k) * P:(UK * g + k + 1) * P])
                        tr = pe.transpose(turned_ps(g)[:, k * SEQ + t * P:k * SEQ + (t + 1) * P], rows, ident[:])
                tr.then_inc(S.tp_ready, 1)

            def turns(n):
                ahead = 2 if n else 1

                def before(u):
                    for g in range(0 if u == 0 else u + ahead, min(u + ahead + 1, GROUPS_N)):
                        turn_group(n, g)
                    pe.wait_ge(S.xT_ready, TURN0[n] + NORM_GAINS[n] * u + 1)
                return before

            def spread_rstd(n):
                if n == 0:
                    pe.wait_ge(S.ones_set, 1)
                k = (0, None, 1, 2, 3)[n]
                pe.wait_ge(S.diag_ready, k + 1)
                for t in range(TT):
                    mm = pe.matmul(side_ps[0][:, t * P:(t + 1) * P], ones[:], diag[:, t, :], start=True, stop=True)
                mm.then_inc(S.spread_done, 1)

            def mem_head(layer, head, step):
                q, kT, v = ((q_A, kT_A, v_A), (q_B, kT_B, v_B))[layer]
                n = HEADS_M * layer + head
                ps = side_ps[0]
                if step == 0:
                    if head == 0:
                        pe.wait_ge(S.chunk_drained, CHUNK0[("qmA", "qmB")[layer]] + 1)
                    if n:
                        pe.wait_ge(S.m_ready, n)
                    if layer == 1 and head == 0:
                        pe.wait_ge(S.spread_ready, 3)
                    for t in range(TT):
                        mm = pe.matmul(ps[:, t * N_MEM:(t + 1) * N_MEM], q[:, head, t * P:(t + 1) * P],
                                       kT[:, head, :], start=True, stop=True)
                    mm.then_inc(S.att_s, 1)
                elif step == 1:
                    pe.wait_ge(S.att_p, n + 1)
                    for k in range(2):
                        for t in range(TT):
                            mm = pe.transpose(ps[:, COLS + k * SEQ + t * P:COLS + k * SEQ + (t + 1) * P],
                                              piece[:, 0, t * N_MEM + k * P:t * N_MEM + (k + 1) * P], ident[:])
                    mm.then_inc(S.att_pt, 1)
                else:
                    pe.wait_ge(S.att_ptc, n + 1)
                    for k in range(2):
                        mm = pe.matmul(ps[:, 0:SEQ], v[:, k, head * P:(head + 1) * P],
                                       piece[:, 1, k * SEQ:(k + 1) * SEQ], start=k == 0, stop=k == 1)
                    mm.then_inc(S.att_o, 1)

            def gates(j, part):
                if part == 0:
                    pe.wait_ge(S.conv_done, j + 1)
                if j + part == 0:
                    pe.wait_ge(S.gates_in, 32)
                if j + part:
                    pe.wait_ge(S.gates_drained, 2 * j + part)
                for g in range(2):
                    for b in range(2):
                        block_n = FT * j + 2 * part + b
                        mm = pe.matmul(side_ps[1][:, g * COLS + b * SEQ:g * COLS + (b + 1) * SEQ],
                                       gw[:, LRU_BLOCKS * g + block_n, :], xc[:, 2 * part + b, :],
                                       start=True, stop=True)
                mm.then_inc(S.gates_done, 1)

            def dil_scores(i):
                pe.wait_ge(S.chunk_drained, CHUNK0["qB"] + min(i, 2) + 1)
                if i == 0:
                    pe.wait_ge(S.m_ready, 2 * HEADS_M)
                else:
                    pe.wait_ge(S.dil_ptc, GROUPS * i)
                for g in range(GROUPS):
                    head = PER_GROUP * g + i
                    q = q_D[:, head_slot(head), :]
                    ps0, ps1 = dil_scores_ps(g)
                    pe.matmul(ps0, q[:, 0:P], kT_D[:, head, 0:P], start=True, stop=True)
                    mm = pe.matmul(ps1, q[:, P:SEQ], kT_D[:, head, :], start=True, stop=True)
                mm.then_inc(S.dil_s, 1)

            def dil_turn(i):
                pe.wait_ge(S.dil_p, i + 1)
                for g in range(GROUPS):
                    ps = dil_pt_ps(g)
                    pe.transpose(ps[:, 0:P], dS[0][:, g * P:(g + 1) * P], ident[:])
                    for k in range(2):
                        mm = pe.transpose(ps[:, (1 + k) * P:(2 + k) * P],
                                          dS[1][:, g * SEQ + k * P:g * SEQ + (k + 1) * P], ident[:])
                    mm.then_inc(S.dil_pt, 1)

            def dil_values(i):
                pe.wait_ge(S.chunk_drained, CHUNK0["vB"] + min(i, 2) + 1)
                pe.wait_ge(S.dil_ptc, GROUPS * PER_GROUP)
                if i:
                    pe.wait_ge(S.d_ready, GROUPS * i)
                for g in range(GROUPS):
                    v = slice(head_slot(PER_GROUP * g + i) * P, (head_slot(PER_GROUP * g + i) + 1) * P)
                    pt = dPT[i][:, g * 384:(g + 1) * 384]
                    pe.matmul(dil_o_ps(g)[:, 0:P], v_D[:, 0, v], pt[:, 0:P], start=True, stop=True)
                    for k in range(2):
                        mm = pe.matmul(dil_o_ps(g)[:, P:SEQ], v_D[:, k, v], pt[:, (1 + k) * P:(2 + k) * P],
                                       start=k == 0, stop=k == 1)
                    mm.then_inc(S.dil_o, 1)

            def pair_of(c):
                return c % 2

            def tiles_of(hi, lo):
                return lambda kt: (hi[:, kt, :], lo[:, kt, :])

            k_all = list(range(KT))
            x_acts, m_acts, mid_acts = tiles_of(xT_hi, xT_lo), tiles_of(mix_hi, mix_lo), tiles_of(mid_hi, mid_lo)

            def mix_B(kt):
                if kt >= HEADS_D:
                    return m_hi_B[:, kt - HEADS_D, :], m_lo_B[:, kt - HEADS_D, :]
                return d_hi[:, head_slot(kt), :], d_lo[:, head_slot(kt), :]

            for c in range(4):
                def after(u, c=c):
                    n = CU * c + u
                    if n == CU - 1:
                        spread_rstd(0)
                    if 14 <= n < 14 + GROUPS_N:
                        turn_group(1, n - 14)
                chunk(CU * c, c, CU * c, pair_of(c), c % 2 == 0, m_acts, k_all, before=turns(0) if c == 0 else None,
                      after=after)

            u0, c0 = UNIT0["qmA"], CHUNK0["qmA"]
            pe.wait_ge(S.xT_ready, TURN0[2])
            chunk(u0, c0, u0, pair_of(c0), True, x_acts, k_all)
            for c in range(len(XG)):
                def after(u, c=c):
                    n = CU * c + u
                    if n % 2 == 0 and 2 <= n <= 24:
                        mem_head(0, (n // 2 - 1) // 3, (n // 2 - 1) % 3)
                    for j, at_unit in enumerate(LRU_AT):
                        if n == at_unit + 2:
                            gates(j, 0)
                        if n == at_unit + 4:
                            gates(j, 1)
                u0, c0 = UNIT0["xg"] + CU * c, CHUNK0["xg"] + c
                chunk(u0, c0, u0, pair_of(c0), True, x_acts, k_all, after=after)

            def wait_mix_A(u):
                if u == 0:
                    pe.wait_ge(S.m_ready, HEADS_M)
                elif u % 2 == 0:
                    pe.wait_ge(S.y_ready, u // 2)

            for c in range(4):
                u0, c0 = UNIT0["outA"] + CU * c, CHUNK0["outA"] + c
                chunk(u0, c0, u0, pair_of(c0), False, m_acts, ORDER_A, before=wait_mix_A if c == 0 else None,
                      tile0_first=True)

            def ffn(layer, norm):
                name = "ffn_in" + layer
                u0, c0 = UNIT0[name], CHUNK0[name]
                chunk(u0, c0, u0, pair_of(c0), True, x_acts, k_all, before=turns(norm))
                spread_rstd(norm)
                chunk(u0 + CU, c0 + 1, u0, pair_of(c0 + 1), True, x_acts, k_all)
                with pe.Fori(1, 11) as i:
                    for c in range(2):
                        chunk(i * (2 * CU) + (u0 + CU * c), i * 2 + (c0 + c), u0, pair_of(c0 + c), True, x_acts, k_all)
                name = "ffn_out" + layer
                u0, c0 = UNIT0[name], CHUNK0[name]
                first_pair = 11 * "AB".index(layer)

                def wait_mid(u):
                    if u % 2 == 0:
                        pe.wait_ge(S.mid_lo_done, first_pair + u // 2 + 1)
                with pe.Fori(0, 2) as i:
                    for c in range(2):
                        chunk(i * (2 * FCU) + (u0 + FCU * c), i * 2 + (c0 + c), u0 + FCU * c, pair_of(c0 + c), False,
                              mid_acts, list(range(FKT)), before=wait_mid if c == 0 else None, tile0_first=True)

            ffn("A", 2)

            u0, c0 = UNIT0["qmB"], CHUNK0["qmB"]
            chunk(u0, c0, u0, pair_of(c0), True, x_acts, k_all, before=turns(3))
            spread_rstd(3)
            pe.wait_ge(S.xT_ready, TURN0[4])
            for c in range(9):
                def after(u, c=c):
                    n = CU * c + u
                    if n % 2 == 0 and 2 <= n <= 24:
                        mem_head(1, (n // 2 - 1) // 3, (n // 2 - 1) % 3)
                    if n in DIL_S:
                        dil_scores(DIL_S.index(n))
                    if n in DIL_PT:
                        dil_turn(DIL_PT.index(n))
                    if n in DIL_O:
                        dil_values(DIL_O.index(n))
                u0, c0 = UNIT0["kB"] + CU * c, CHUNK0["kB"] + c
                chunk(u0, c0, u0, pair_of(c0), c < 6, x_acts if 3 <= c < 6 else m_acts, k_all, after=after)

            def wait_mix_B(u):
                if u == 0:
                    pe.wait_ge(S.m_ready, 2 * HEADS_M)
                elif u >= 2:
                    pe.wait_ge(S.d_ready, GROUPS * -(-(2 * u - 2) // GROUPS))

            def last_trios(u):
                n = 9 * CU + u
                if n in DIL_O:
                    dil_values(DIL_O.index(n))

            for c in range(4):
                u0, c0 = UNIT0["outB"] + CU * c, CHUNK0["outB"] + c
                chunk(u0, c0, u0, pair_of(c0), False, mix_B, ORDER_B, before=wait_mix_B if c == 0 else None,
                      after=last_trios if c == 0 else None, tile0_first=True)
            ffn("B", 4)

        @block.scalar
        def _(act):
            def split(n, slot, first_use=False):
                act.wait_ge(landed[slot], n_landed(n, slot))
                if not first_use:
                    act.wait_ge(S.unit_used, n + (1 - RING))
                act.activation(w_hi[:, slot, :], raw[:, slot, :], ACT.Copy).then_inc(S.hi_done, 1)

            def n_landed(n, slot):
                if isinstance(n, int):
                    return 16 * (n // RING + 1)
                return n * 4 + (16 - 4 * slot)

            def split_range(n0, count):
                turns = count // RING if count > 2 * RING else 0
                if turns:
                    with act.Fori(0, turns) as i:
                        for u in range(RING):
                            split(i * RING + (n0 + u), (n0 + u) % RING)
                for n in range(n0 + turns * RING, n0 + count):
                    split(n, n % RING, n < RING)

            def norm_squares(n, t):
                src, _ = norm_plan(n)
                if n + t:
                    act.wait_ge(S.sq_summed, TT * n + t)
                if n == 0:
                    for q in range(4):
                        act.wait_ge(mem_in[q], 16)
                elif n == 1:
                    act.wait_ge(S.x_in, 64)
                else:
                    act.wait_ge(S.h_new, GROUPS_N * TT * (n - 1))
                scraps, rows = ((small.rearrange("p (a b) -> p a b", a=4), src[:, :, t, :]) if n == 0 else
                                (small, src[:, t, :]))
                act.activation(scraps, rows, ACT.Square, accum_out=ssq(n)[:, t:t + 1]).then_inc(S.sq_summed, 1)

            def norm_std(k):
                act.wait_ge(S.var_ready, k + 1)
                act.activation(st[:, 56:58], st[:, 54:56], ACT.Sqrt).then_inc(S.std_ready, 1)

            def load_sqrt():
                act.activation(scrap1, one, ACT.Sqrt)

            def x_rows(q):
                if q == 0:
                    act.wait_ge(S.rstd_ready, 1)
                if q >= 2:
                    act.wait_ge(S.tp_ready, GROUP0[1] + 2 * (q - 1))
                for t in range(TT):
                    ins = act.activation(piece[:, q % 2, t * COLS:(t + 1) * COLS], h[:, t, q * COLS:(q + 1) * COLS],
                                         ACT.Copy, scale=rstd(1)[:, t:t + 1])
                ins.then_inc(S.hn_ready, 1)

            def turned_hi(n, g):
                _, targets = norm_plan(n)
                act.wait_ge(S.tp_ready, GROUP0[n] + g + 1)
                for row, hi_to, _ in targets:
                    for k in range(UK):
                        kt = UK * g + k
                        ins = act.activation(hi_to[:, kt, :], turned_ps(g)[:, k * SEQ:(k + 1) * SEQ], ACT.Copy,
                                             scale=gain[:, row, kt:kt + 1])
                ins.then_inc(S.xhi_ready, 1)

            def copy_spread(k):
                act.wait_ge(S.spread_done, k + 1)
                act.activation(spread[:], side_ps[0][:, 0:SEQ], ACT.Copy).then_inc(S.spread_ready, 1)

            def turned_chunk(n, k, u0):
                for g in range(GROUPS_N):
                    if n == 0:
                        split(g, g % RING, g < RING)
                    turned_hi(n, g)
                    if n and 1 <= g <= 5:
                        split(u0 + g + 2, (u0 + g + 2) % RING)
                    if n == 0 and g >= 4:
                        cols = slice((g - 4) * COLS, (g - 3) * COLS)
                        act.dma_start(h[:, :, cols], x[:, cols].rearrange("(t p) n -> p t n", p=P)).then_inc(S.x_in, 16)
                    if g >= GROUPS_N - TT:
                        norm_squares(n, g - (GROUPS_N - TT))
                norm_std(k)

            def drain(c, dst):
                act.wait_ge(S.unit_used, units_by(c + 1))
                act.activation(dst, gemm_ps[c % 2][:], ACT.Copy).then_inc(S.chunk_drained, 1)

            def drain_values(c, dst, n):
                act.wait_ge(S.unit_used, units_by(c + 1))
                for t in range(TT):
                    ins = act.activation(dst[:, t, :], gemm_ps[c % 2][:, t * COLS:(t + 1) * COLS], ACT.Copy,
                                         scale=rstd(n)[:, t:t + 1])
                ins.then_inc(S.chunk_drained, 1)

            def y_squares(name, c, t):
                s = TOKEN_STAGES.index(name)
                if t == 0:
                    act.wait_ge(S.tile0_done, 4 * s + c + 1)
                    if s + c:
                        act.wait_ge(S.y_squared, TT * (4 * s + c))
                else:
                    act.wait_ge(S.unit_used, units_by(CHUNK0[name] + c + 1))
                act.activation(token_buffers(name)[2][:, t * COLS:(t + 1) * COLS],
                               gemm_ps[(CHUNK0[name] + c) % 2][:, t * COLS:(t + 1) * COLS], ACT.Square,
                               accum_out=y_ssq(name)[:, 2 * c + t:2 * c + t + 1]).then_inc(S.y_squared, 1)

            def mem_softmax(layer, head):
                n = HEADS_M * layer + head
                act.wait_ge(S.att_mx, n + 1)
                for t in range(TT):
                    ins = act.activation(piece[:, 0, t * N_MEM:(t + 1) * N_MEM],
                                         side_ps[0][:, t * N_MEM:(t + 1) * N_MEM], ACT.Exp,
                                         bias=nmx[:, t:t + 1], scale=SCALE, accum_out=zz[:, t:t + 1])
                ins.then_inc(S.att_exp, 1)

            def mem_react(layer, slot):
                head, stp = slot // 3, slot % 3
                n = HEADS_M * layer + head
                if stp == 0:
                    mem_softmax(layer, head)
                elif stp == 1:
                    act.wait_ge(S.att_pt, n + 1)
                    act.activation(piece[:, 1, 0:COLS], side_ps[0][:, COLS:2 * COLS], ACT.Copy).then_inc(S.att_ptc, 1)
                else:
                    act.wait_ge(S.att_o, n + 1)
                    to = m_hi_B[:, head, :] if layer else mix_hi[:, HEADS_D + head, :]
                    act.activation(to, side_ps[0][:, 0:SEQ], ACT.Copy).then_inc(S.m_hi, 1)

            def gate_sigmoids(j, part):
                act.wait_ge(S.gates_done, 2 * j + part + 1)
                if part == 0 and j:
                    act.wait_ge(S.scan_done, j)
                for g, dst in enumerate((rr, ii)):
                    for b in range(2):
                        k = 2 * part + b
                        ins = act.activation(dst[:, k, :], side_ps[1][:, g * COLS + b * SEQ:g * COLS + (b + 1) * SEQ],
                                             ACT.Sigmoid, bias=lr[:, 5 + g, FT * j + k:FT * j + k + 1])
                ins.then_inc(S.gates_drained, 1)

            def decays(j, part):
                act.wait_ge(S.gates_drained, 2 * j + part + 1)
                if j == 0:
                    act.wait_ge(S.lru_c, 1)
                else:
                    act.wait_ge(S.scan_y, j)
                for b in range(2 * part, 2 * part + 2):
                    k = FT * j + b
                    act.activation(bb[:, b, :], rr[:, b, :], ACT.Tanh, scale=lc[:, 1, k:k + 1])
                    ins = act.activation(aa[:, b, :], rr[:, b, :], ACT.Exp, scale=lc[:, 0, k:k + 1])
                ins.then_inc(S.decay_ready, 1)

            def root(j):
                act.wait_ge(S.ratio_ready, j + 1)
                act.activation(flat(rr[:]), flat(bb[:]), ACT.Sqrt, bias=tiny).then_inc(S.sqrt_done, 1)

            def y_hi_part(j):
                act.wait_ge(S.scan_y, j + 1)
                act.activation(flat(mix_hi[:, FT * j:FT * j + FT, :]), flat(ge[:]), ACT.Copy).then_inc(S.y_hi, 1)

            def copy_xb(j, c):
                act.wait_ge(S.unit_used, units_by(c + 1))
                if j:
                    act.wait_ge(S.conv_done, j)
                act.activation(xbp[:, :, TAPS - 1:], gemm_ps[c % 2][:].rearrange("p (a b) -> p a b", a=FT), ACT.Copy
                               ).then_inc(S.chunk_drained, 1)

            def gelu(j, c):
                act.wait_ge(S.unit_used, units_by(c + 1))
                if j:
                    act.wait_ge(S.y_ready, j)
                act.activation(flat(ge[:]), gemm_ps[c % 2][:], ACT.Gelu_apprx_tanh).then_inc(S.chunk_drained, 1)

            act.dma_start(ident[:], ident_in).then_inc(S.consts_in, 16)
            act.dma_start(flat(gain[:]), gains).then_inc(S.consts_in, 16)
            act.wait_ge(S.one_set, 1)
            load_sqrt()
            act.wait_ge(S.consts_in, 32)
            turned_chunk(0, 0, 0)
            for n in range(CU, UNIT0["xg"]):
                split_range(n, 1)
                if n == 11:
                    copy_spread(0)
                    act.wait_ge(S.lru_abs, 1)
                    act.activation(lc[:, 2, :], lc[:, 2, :], ACT.Exp, scale=-1.0).then_inc(S.lru_ez, 1)
                if n in (11, 12):
                    norm_squares(1, n - 11)
                if n == 13:
                    norm_std(1)
                if n in (14, 16, 18, 20):
                    x_rows((n - 14) // 2)
                if 18 <= n < 18 + GROUPS_N:
                    turned_hi(1, n - 18)
                if n == 19:
                    drain_values(1, v_A, 0)
                if n == 35:
                    drain_values(3, v_B, 0)

            for n in range(7 * CU):
                split_range(UNIT0["xg"] + n, 1)
                if n == 3:
                    drain(CHUNK0["qmA"], flat(q_A[:]))
                if n % 2 == 0 and 6 <= n <= 28:
                    mem_react(0, n // 2 - 3)
                for c, (branch, j) in enumerate(XG):
                    if branch == "x" and n == LRU_AT[j]:
                        copy_xb(j, CHUNK0["xg"] + c)
                    if branch == "g" and n == CU * (c + 1) + 3:
                        gelu(j, CHUNK0["xg"] + c)
                for j, at_unit in enumerate(LRU_AT):
                    if n == at_unit + 6:
                        gate_sigmoids(j, 0)
                    if n == at_unit + 8:
                        gate_sigmoids(j, 1)
                    if n in (at_unit + 9, at_unit + 10):
                        decays(j, n - at_unit - 9)
                    if n == at_unit + 11:
                        root(j)
                    if n == Y_AT[j]:
                        y_hi_part(j)

            def token_stage(name, units):
                for c in range(1, 4):
                    n0 = UNIT0[name] + units * c
                    split_range(n0, 4)
                    for t in range(TT):
                        y_squares(name, c - 1, t)
                    split_range(n0 + 4, units - 4)

            def post_norm(name, k, norm, next_unit):
                load_sqrt()
                split_range(next_unit, 2)
                y_squares(name, 3, 0)
                split(next_unit + 2, (next_unit + 2) % RING)
                y_squares(name, 3, 1)
                norm_std(k)
                turned_chunk(norm, k + 1, next_unit)

            def mid_hi_part(k, at_tile):
                act.wait_ge(S.hid_ready, k)
                act.activation(flat(mid_hi[:, at_tile, :]), piece[:, 1, :], ACT.Copy).then_inc(S.mid_hi_done, 1)

            def ffn_in(layer):
                name = "ffn_in" + layer
                u0 = UNIT0[name]
                k0 = 11 * "AB".index(layer)

                def one(i, first):
                    if not first:
                        for u in range(4):
                            split(i * 16 + (u0 + u), u)
                        mid_hi_part(i + k0, bass.ds(i * FT - FT, FT))
                        for u in range(4, 8):
                            split(i * 16 + (u0 + u), u % RING)
                    for u in range(8, 12):
                        split(i * 16 + (u0 + u), u % RING)
                    if first:
                        copy_spread(1 + 2 * "AB".index(layer))
                    act.wait_ge(S.chunk_drained, i * 2 + (CHUNK0[name] + 1))
                    act.activation(piece[:, 0, :], piece[:, 0, :], ACT.Silu).then_inc(S.silu_done, 1)
                    for u in range(12, 16):
                        split(i * 16 + (u0 + u), u % RING)
                one(0, True)
                with act.Fori(1, 11) as i:
                    one(i, False)
                n0 = UNIT0["ffn_out" + layer]
                split_range(n0, 4)
                mid_hi_part(k0 + 11, slice(FKT - FT, FKT))
                split_range(n0 + 4, FCU - 4)

            token_stage("outA", CU)
            post_norm("outA", 2, 2, UNIT0["ffn_inA"])
            ffn_in("A")
            token_stage("ffn_outA", FCU)
            post_norm("ffn_outA", 4, 3, UNIT0["qmB"])

            def dil_exp(i):
                act.wait_ge(S.dil_mx, i + 1)
                for t in range(TT):
                    ins = act.activation(dS[t], dS[t], ACT.Exp, bias=nmx[:, t:t + 1], scale=SCALE,
                                         accum_out=zz[:, t:t + 1])
                ins.then_inc(S.dil_exp, 1)

            for n in range(10 * CU):
                split_range(UNIT0["kB"] + n, 1)
                if n == 3:
                    copy_spread(2)
                if n % 2 == 0 and 6 <= n <= 28:
                    mem_react(1, n // 2 - 3)
                for c in range(3):
                    if n == CU * (7 + c) + 3:
                        drain_values(CHUNK0["vB"] + c, v_D[:, :, c * COLS:(c + 1) * COLS], 3)
                if n - 4 in DIL_S:
                    dil_exp(DIL_S.index(n - 4))
                if n - 4 in DIL_PT:
                    i = DIL_PT.index(n - 4)
                    for g in range(GROUPS):
                        act.wait_ge(S.dil_pt, GROUPS * i + g + 1)
                        act.activation(dPT[i][:, g * 384:(g + 1) * 384], dil_pt_ps(g), ACT.Copy).then_inc(S.dil_ptc, 1)
                if n - 4 in DIL_O:
                    i = DIL_O.index(n - 4)
                    for g in range(GROUPS):
                        act.wait_ge(S.dil_o, GROUPS * i + g + 1)
                        act.activation(d_hi[:, GROUPS * i + g, :], dil_o_ps(g), ACT.Copy).then_inc(S.d_hi, 1)
            token_stage("outB", CU)
            post_norm("outB", 6, 4, UNIT0["ffn_inB"])
            ffn_in("B")
            token_stage("ffn_outB", FCU)
            load_sqrt()
            for t in range(TT):
                y_squares("ffn_outB", 3, t)
            norm_std(8)

        @block.vector
        def _(dve):
            steps = [0]

            def step(ins):
                steps[0] += 1
                ins.then_inc(S.dve_step, 1)
                dve.wait_ge(S.dve_step, steps[0])

            def split(n, slot):
                dve.wait_ge(S.hi_done, n + 1)
                dve.tensor_tensor(w_lo[:, slot, :], raw[:, slot, :], w_hi[:, slot, :].bitcast(F32), ALU.subtract
                                  ).then_inc(S.lo_done, 1)

            def split_range(n0, count):
                turns = count // RING if count > 2 * RING else 0
                if turns:
                    with dve.Fori(0, turns) as i:
                        for u in range(RING):
                            split(i * RING + (n0 + u), (n0 + u) % RING)
                for n in range(n0 + turns * RING, n0 + count):
                    split(n, n % RING)

            def lo_part(dst, whole, hi):
                return dve.tensor_tensor(dst, whole, hi, ALU.subtract)

            def variance(src):
                dve.tensor_scalar(st[:, 54:56], src, 1.0 / D, EPS, ALU.mult, ALU.add).then_inc(S.var_ready, 1)

            def norm_var(n):
                dve.wait_ge(S.sq_summed, TT * (n + 1))
                variance(ssq(n))

            def norm_rstd(n, k):
                dve.wait_ge(S.std_ready, k + 1)
                dve.reciprocal(rstd(n), st[:, 56:58]).then_inc(S.rstd_ready, 1)

            def rstd_diag(n):
                for t in range(TT):
                    ins = dve.tensor_scalar(diag[:, t, :], ident[:], rstd(n)[:, t:t + 1], None, ALU.mult)
                ins.then_inc(S.diag_ready, 1)

            def turned_lo(n, g):
                _, targets = norm_plan(n)
                dve.wait_ge(S.xhi_ready, GROUP0[n] + g + 1)
                for row, hi_to, lo_to in targets:
                    for k in range(UK):
                        kt = UK * g + k
                        ins = dve.scalar_tensor_tensor(lo_to[:, kt, :], turned_ps(g)[:, k * SEQ:(k + 1) * SEQ],
                                                       gain[:, row, kt:kt + 1], hi_to[:, kt, :].bitcast(F32), ALU.mult,
                                                       ALU.subtract)
                    ins.then_inc(S.xT_ready, 1)

            def turned_chunk(n, k, u0, name=None):
                for g in range(3 if n else 0):
                    residual(name, g)
                for g in range(GROUPS_N):
                    if n == 0:
                        split(g, g % RING)
                    turned_lo(n, g)
                    if n and g == 1:
                        y_scale(name, 3, 1)
                        dve.wait_ge(S.chunk_drained, CHUNK0[name] + 4)
                    if n and g <= 5:
                        split(u0 + g + 2, (u0 + g + 2) % RING)
                    if n and g + 3 < GROUPS_N:
                        residual(name, g + 3)
                norm_var(n)
                dve.wait_ge(S.std_ready, k + 1)
                step(dve.reciprocal(rstd(n), st[:, 56:58]))
                rstd_diag(n)

            def drain(c, dst):
                k = 1 if c < CHUNK0["qmA"] else 3
                dve.wait_ge(S.spread_ready, k)
                dve.wait_ge(S.unit_used, units_by(c + 1))
                dve.tensor_tensor(dst, gemm_ps[c % 2][:].rearrange("p (a b) -> p a b", a=FT),
                                  spread[:].unsqueeze(1).to_broadcast([P, FT, SEQ]), ALU.mult
                                  ).then_inc(S.chunk_drained, 1)

            def y_scale(name, c, t):
                s = TOKEN_STAGES.index(name)
                y_to, g, _ = token_buffers(name)
                dve.wait_ge(S.post_g_in, 16 * (s + 1))
                dve.wait_ge(S.y_squared, TT * (4 * s + c) + t + 1)
                ins = dve.tensor_tensor(
                    y_to[:, 2 * c:2 * c + 2, t, :],
                    gemm_ps[(CHUNK0[name] + c) % 2][:, t * COLS:(t + 1) * COLS].rearrange("p (a b) -> p a b", a=2),
                    g[:, c * COLS:(c + 1) * COLS].rearrange("p (a b) -> p a b", a=2), ALU.mult)
                if t == TT - 1:
                    ins.then_inc(S.chunk_drained, 1)

            def y_norm(name, k):
                s = TOKEN_STAGES.index(name)
                dve.wait_ge(S.y_squared, TT * 4 * (s + 1))
                step(dve.tensor_reduce(st[:, 42:44], y_ssq(name).rearrange("p (c t) -> p t c", t=TT), AX.X, ALU.add))
                variance(st[:, 42:44])
                dve.wait_ge(S.chunk_drained, CHUNK0[name] + 3)
                dve.wait_ge(S.std_ready, k + 1)
                step(dve.reciprocal(y_rstd(), st[:, 56:58]))

            def residual(name, g, groups=1):
                cols = slice(g * UK * P, (g + groups) * UK * P)
                for t in range(TT):
                    a, b = token_buffers(name)[0][:, g:g + groups, t, :], h[:, t, cols]
                    if groups == 1:
                        a = a.rearrange("p a b -> p (a b)")
                    else:
                        b = b.rearrange("p (a b) -> p a b", a=groups)
                    dve.scalar_tensor_tensor(b, a, y_rstd()[:, t:t + 1], b, ALU.mult, ALU.add).then_inc(S.h_new, 1)

            def mem_react(layer, slot):
                head, stp = slot // 3, slot % 3
                n = HEADS_M * layer + head
                if stp == 0:
                    dve.wait_ge(S.att_s, n + 1)
                    step(dve.tensor_reduce(mx, side_ps[0][:, 0:COLS].rearrange("p (t n) -> p t n", t=TT), AX.X,
                                           ALU.max))
                    dve.tensor_scalar(nmx, mx, -SCALE, None, ALU.mult).then_inc(S.att_mx, 1)
                    dve.wait_ge(S.att_exp, n + 1)
                    step(dve.reciprocal(rz, zz))
                    for t in range(TT):
                        p = piece[:, 0, t * N_MEM:(t + 1) * N_MEM]
                        ins = dve.tensor_scalar(p, p, rz[:, t:t + 1], None, ALU.mult)
                    ins.then_inc(S.att_p, 1)
                elif stp == 2:
                    dve.wait_ge(S.m_hi, n + 1)
                    to, hi = ((m_lo_B[:, head, :], m_hi_B[:, head, :]) if layer else
                              (mix_lo[:, HEADS_D + head, :], mix_hi[:, HEADS_D + head, :]))
                    lo_part(to, side_ps[0][:, 0:SEQ], hi.bitcast(F32)).then_inc(S.m_ready, 1)

            def conv(j, k):
                if k == TAPS - 1:
                    c = CHUNK0["xg"] + XG.index(("x", j))
                    dve.wait_ge(S.chunk_drained, c + 1)
                    if j == 0:
                        dve.wait_ge(S.pads_zero, 1)
                else:
                    dve.wait_ge(S.tap_done, (TAPS - 1) * j + TAPS - 1 - k)
                for b in range(FT):
                    n = FT * j + b
                    w = lr[:, k, n:n + 1]
                    src = xbp[:, b, k:k + SEQ]
                    if k == TAPS - 1:
                        ins = dve.tensor_scalar(xc[:, b, :], src, w, lr[:, 4, n:n + 1], ALU.mult, ALU.add)
                    else:
                        ins = dve.scalar_tensor_tensor(xc[:, b, :], src, w, xc[:, b, :], ALU.mult, ALU.add)
                ins.then_inc(S.tap_done if k else S.conv_done, 1)

            def lru_input(j):
                dve.wait_ge(S.gates_drained, 2 * j + 2)
                step(dve.tensor_tensor(flat(ii[:]), flat(ii[:]), flat(xc[:]), ALU.mult))

            def lru_ratio(j):
                dve.wait_ge(S.decay_ready, 2 * (j + 1))
                step(dve.tensor_tensor(flat(rr[:]), flat(aa[:]), flat(aa[:]), ALU.mult))
                dve.scalar_tensor_tensor(flat(bb[:]), flat(rr[:]), 1.0, flat(bb[:]), ALU.add, ALU.mult
                                         ).then_inc(S.ratio_ready, 1)

            def lru_scan(j):
                dve.wait_ge(S.sqrt_done, j + 1)
                step(dve.tensor_tensor(flat(bb[:]), flat(rr[:]), flat(ii[:]), ALU.mult))
                for b in range(FT):
                    ins = dve.tensor_tensor_scan(bb[:, b, :], aa[:, b, :], bb[:, b, :], 0.0, ALU.mult, ALU.add)
                ins.then_inc(S.scan_done, 1)

            def lru_out(j):
                dve.wait_ge(S.scan_done, j + 1)
                dve.wait_ge(S.chunk_drained, CHUNK0["xg"] + XG.index(("g", j)) + 1)
                dve.tensor_tensor(flat(ge[:]), flat(bb[:]), flat(ge[:]), ALU.mult).then_inc(S.scan_y, 1)
                dve.wait_ge(S.y_hi, j + 1)
                lo_part(flat(mix_lo[:, FT * j:FT * j + FT, :]), flat(ge[:]),
                        flat(mix_hi[:, FT * j:FT * j + FT, :]).bitcast(F32)).then_inc(S.y_ready, 1)

            def decay_constants():
                lam, z, s, s2, acc, t = (lr[:, 7, :], lc[:, 2, :], lc[:, 3, :], lc[:, 4, :], lc[:, 5, :], lc[:, 6, :])
                dve.wait_ge(S.lru_ez, 1)
                step(dve.tensor_scalar(t, z, 2.0, None, ALU.add))
                step(dve.reciprocal(t, t))
                step(dve.tensor_tensor(s, z, t, ALU.mult))
                step(dve.tensor_tensor(s2, s, s, ALU.mult))
                top = 17
                step(dve.tensor_scalar(acc, s2, 1.0 / top, 1.0 / (top - 2), ALU.mult, ALU.add))
                for k in range(top - 4, 0, -2):
                    step(dve.tensor_tensor(acc, acc, s2, ALU.mult))
                    step(dve.tensor_scalar(acc, acc, 1.0 / k, None, ALU.add))
                step(dve.tensor_tensor(acc, acc, s, ALU.mult))
                step(dve.tensor_scalar(t, lam, -1.0, 0.0, ALU.mult, ALU.max))
                step(dve.scalar_tensor_tensor(t, acc, 2.0, t, ALU.mult, ALU.add))
                step(dve.tensor_scalar(lc[:, 0, :], t, -LRU_C, None, ALU.mult))
                dve.tensor_scalar(lc[:, 1, :], t, LRU_C, None, ALU.mult).then_inc(S.lru_c, 1)

            dve.memset(one, 1.0)
            dve.memset(tiny, 1e-30).then_inc(S.one_set, 1)
            dve.wait_ge(S.consts_in, 32)
            turned_chunk(0, 0, 0)
            dve.wait_ge(S.lru_in, 16)
            lam = lr[:, 7, :]
            step(dve.tensor_scalar(lc[:, 7, :], lam, -1.0, None, ALU.mult))
            dve.tensor_tensor(lc[:, 2, :], lc[:, 7, :], lam, ALU.max).then_inc(S.lru_abs, 1)
            for n in range(CU, UNIT0["xg"]):
                split_range(n, 1)
                if n == 11:
                    drain(0, kT_A[:])
                if n == 12:
                    norm_var(1)
                if n == 13:
                    norm_rstd(1, 1)
                if 18 <= n < 18 + GROUPS_N:
                    turned_lo(1, n - 18)
                if n == 27:
                    drain(2, kT_B)
                if n == 30:
                    decay_constants()

            for n in range(7 * CU):
                split_range(UNIT0["xg"] + n, 1)
                if n % 2 == 0 and 6 <= n <= 28:
                    mem_react(0, n // 2 - 3)
                for j, at_unit in enumerate(LRU_AT):
                    if at_unit <= n < at_unit + TAPS:
                        conv(j, TAPS - 1 - (n - at_unit))
                    if n == at_unit + 9:
                        lru_input(j)
                    if n == at_unit + 10:
                        lru_ratio(j)
                    if n == at_unit + 12:
                        lru_scan(j)
                    if n == Y_AT[j]:
                        lru_out(j)

            def token_stage(name, units):
                for c in range(1, 4):
                    n0 = UNIT0[name] + units * c
                    split_range(n0, 4)
                    for t in range(TT):
                        y_scale(name, c - 1, t)
                    split_range(n0 + 4, units - 4)

            def post_norm(name, k, norm, next_unit):
                split_range(next_unit, 2)
                y_scale(name, 3, 0)
                y_norm(name, k)
                turned_chunk(norm, k + 1, next_unit, name)

            def ffn_in(layer):
                name = "ffn_in" + layer
                u0, c0 = UNIT0[name], CHUNK0[name]
                k0 = 11 * "AB".index(layer)

                def scaled(to, c, u):
                    dve.wait_ge(S.unit_used, u)
                    dve.tensor_tensor(piece[:, to, :].rearrange("p (a b) -> p a b", a=FT),
                                      gemm_ps[(c0 + to) % 2][:].rearrange("p (a b) -> p a b", a=FT),
                                      spread[:].unsqueeze(1).to_broadcast([P, FT, SEQ]), ALU.mult
                                      ).then_inc(S.chunk_drained, 1)

                def hidden(k, c, u, at_tile):
                    if not isinstance(k, int) or k > 1:
                        dve.wait_ge(S.mid_lo_done, k - 1)
                    scaled(1, c, u)
                    dve.wait_ge(S.chunk_drained, c)
                    dve.wait_ge(S.silu_done, k)
                    dve.tensor_tensor(piece[:, 1, :], piece[:, 1, :], piece[:, 0, :], ALU.mult).then_inc(S.hid_ready, 1)
                    dve.wait_ge(S.mid_hi_done, k)
                    lo_part(flat(mid_lo[:, at_tile, :]), piece[:, 1, :], flat(mid_hi[:, at_tile, :]).bitcast(F32)
                            ).then_inc(S.mid_lo_done, 1)

                def one(i, first):
                    if not first:
                        for u in range(4):
                            split(i * 16 + (u0 + u), u)
                        hidden(i + k0, i * 2 + c0, i * 16 + u0,
                               slice(0, FT) if isinstance(i, int) else bass.ds(i * FT - FT, FT))
                        for u in range(4, 8):
                            split(i * 16 + (u0 + u), u % RING)
                    for u in range(8, 12):
                        split(i * 16 + (u0 + u), u % RING)
                    if first:
                        dve.wait_ge(S.spread_ready, (2, 4)["AB".index(layer)])
                    scaled(0, i * 2 + c0, i * 16 + (u0 + CU))
                    for u in range(12, 16):
                        split(i * 16 + (u0 + u), u % RING)
                one(0, True)
                one(1, False)
                with dve.Fori(2, 11) as i:
                    one(i, False)
                n0 = UNIT0["ffn_out" + layer]
                split_range(n0, 4)
                hidden(k0 + 11, c0 + 22, n0, slice(FKT - FT, FKT))
                split_range(n0 + 4, FCU - 4)

            token_stage("outA", CU)
            post_norm("outA", 2, 2, UNIT0["ffn_inA"])
            ffn_in("A")
            token_stage("ffn_outA", FCU)
            post_norm("ffn_outA", 4, 3, UNIT0["qmB"])

            def dil_softmax(i):
                dve.wait_ge(S.dil_s, i + 1)
                if i == 0:
                    dve.wait_ge(S.far_in, 16)
                else:
                    dve.wait_ge(S.dil_pt, GROUPS * i)
                for g in range(GROUPS):
                    slope = -(2.0 ** (-8.0 * (PER_GROUP * g + i + 1) / HEADS_D)) / SCALE
                    ps0, ps1 = dil_scores_ps(g)
                    dve.scalar_tensor_tensor(dS[0][:, g * P:(g + 1) * P], far[:, g, P:2 * P], slope, ps0, ALU.mult,
                                             ALU.add)
                    ins = dve.scalar_tensor_tensor(dS[1][:, g * SEQ:(g + 1) * SEQ], far[:, g, :], slope, ps1, ALU.mult,
                                                   ALU.add)
                step(ins)
                dve.tensor_reduce(mx[:, 0:1], dS[0], AX.X, ALU.max)
                step(dve.tensor_reduce(mx[:, 1:2], dS[1], AX.X, ALU.max))
                dve.tensor_scalar(nmx, mx, -SCALE, None, ALU.mult).then_inc(S.dil_mx, 1)
                dve.wait_ge(S.dil_exp, i + 1)
                step(dve.reciprocal(rz, zz))
                for t in range(TT):
                    ins = dve.tensor_scalar(dS[t], dS[t], rz[:, t:t + 1], None, ALU.mult)
                ins.then_inc(S.dil_p, 1)

            for n in range(10 * CU):
                split_range(UNIT0["kB"] + n, 1)
                if n == 3:
                    drain(CHUNK0["qmB"], q_B[:])
                if n % 2 == 0 and 6 <= n <= 28:
                    mem_react(1, n // 2 - 3)
                for c in range(3):
                    if n == CU * (1 + c) + 3:
                        drain(CHUNK0["kB"] + c, kT_D[:, FT * c:FT * c + FT, :])
                    if n == CU * (4 + c) + 3:
                        drain(CHUNK0["qB"] + c, q_D[:, FT * c:FT * c + FT, :])
                if n - 4 in DIL_S:
                    dil_softmax(DIL_S.index(n - 4))
                if n - 4 in DIL_O:
                    i = DIL_O.index(n - 4)
                    for g in range(GROUPS):
                        dve.wait_ge(S.d_hi, GROUPS * i + g + 1)
                        lo_part(d_lo[:, GROUPS * i + g, :], dil_o_ps(g), d_hi[:, GROUPS * i + g, :].bitcast(F32)
                                ).then_inc(S.d_ready, 1)
            token_stage("outB", CU)
            post_norm("outB", 6, 4, UNIT0["ffn_inB"])
            ffn_in("B")
            token_stage("ffn_outB", FCU)
            y_scale("ffn_outB", 3, 0)
            y_norm("ffn_outB", 8)
            for q in range(4):
                if q == 1:
                    y_scale("ffn_outB", 3, 1)
                if q == 3:
                    dve.wait_ge(S.chunk_drained, CHUNK0["ffn_outB"] + 4)
                residual("ffn_outB", 2 * q, 2)


def tiles(w, k_order, cols):
    out = []
    for c in cols:
        block = w[:, c:c + COLS].reshape(-1, P, COLS)[k_order]
        block = block.reshape(-1, UK, P, COLS).transpose(0, 2, 1, 3)
        out.append(block.reshape(-1, P, UNIT))
    return out


def by_trio(w):
    return w.reshape(len(w), HEADS_D, P)[:, TRIO_HEADS].reshape(len(w), -1)


def by_partition(v):
    return v.reshape(-1, P).T


def kernel(**inputs):
    import concourse.bacc as bacc
    from concourse.bass_utils import run_bass_kernel_spmd

    a = {k: np.asarray(v) for k, v in inputs.items()}
    d_all, f_all = list(range(KT)), list(range(FKT))
    units = []
    units += tiles(a["a_w_mem_kv"][0], d_all, (0, 512))
    units += tiles(a["b_w_mem_kv"][0], d_all, (0, 512))
    units += tiles(a["a_w_in"][0], d_all, (3072, *(512 * j + (1536 if branch == "g" else 0) for branch, j in XG)))
    units += tiles(a["a_w_out"][0], ORDER_A, range(0, D, COLS))
    pairs = [c for j in range(0, D_FF, COLS) for c in (j, D_FF + j)]
    units += tiles(a["a_w_ffn_in"][0], d_all, pairs)
    units += tiles(a["a_w_ffn_out"][0], f_all, range(0, D, COLS))
    units += tiles(a["b_w_in"][0], d_all, (1536,))
    units += tiles(a["w_kv_shared"], d_all, (0, 512, 1024))
    units += tiles(by_trio(a["b_w_in"][0][:, :HEADS_D * P]), d_all, (0, 512, 1024))
    units += tiles(by_trio(a["w_kv_shared"][:, HEADS_D * P:]), d_all, (0, 512, 1024))
    units += tiles(a["b_w_out"][0], ORDER_B, range(0, D, COLS))
    units += tiles(a["b_w_ffn_in"][0], d_all, pairs)
    units += tiles(a["b_w_ffn_out"][0], f_all, range(0, D, COLS))
    stream = np.concatenate(units)

    gains = np.concatenate([by_partition(v) for v in (
        a["mem_norm_g"], a["a_pre_mix_g"][0], a["a_pre_ffn_g"][0], a["kv_norm_g"], a["b_pre_mix_g"][0],
        a["b_pre_ffn_g"][0])], axis=1)
    lru = np.concatenate([by_partition(v) for v in (
        *a["a_conv_w"][0], a["a_conv_b"][0], a["a_gate_a_b"][0], a["a_gate_x_b"][0], a["a_lambda"][0])], axis=1)
    gate_w = np.concatenate([a["a_gate_a_w"][0], a["a_gate_x_w"][0]]).transpose(1, 0, 2).reshape(P, -1)
    post_g = np.stack([a["a_post_mix_g"][0], a["a_post_ffn_g"][0], a["b_post_mix_g"][0], a["b_post_ffn_g"][0]])

    rel = np.arange(P)[:, None] + P - np.arange(2 * P)[None, :]
    dist = np.stack([np.where((rel >= 0) & (rel % d == 0) & ((rel <= P) if d == 1 else True), rel, FAR)
                     for d in DIL], axis=1).reshape(P, -1).astype(np.float32)
    arrays = {"stream": stream, "x": a["x"][0], "mem": a["mem"][0], "gains": gains, "lru": lru, "gate_w": gate_w,
              "post_g": post_g, "dist": dist, "ident": np.eye(P, dtype=np.float32)}
    arrays = {k: np.ascontiguousarray(v) for k, v in arrays.items()}

    nc = bacc.Bacc("TRN2", target_bir_lowering=False, num_devices=1)
    args = [nc.dram_tensor(k, v.shape, mybir.dt.from_np(v.dtype), kind="ExternalInput").ap() for k, v in arrays.items()]
    args.append(nc.dram_tensor("out", (SEQ, D), F32, kind="ExternalOutput").ap())
    build(nc, *args)
    r = run_bass_kernel_spmd(nc, [arrays], core_ids=[0])
    return r.results[0]["out"].reshape(1, SEQ, D)
```
